# Optimizing a Trainium2 kernel written in Bass

```python
import jax, jax.numpy as jnp
from jax import lax
import numpy as np

D_MODEL = 1024
BATCH = 1
SEQ = 2048
DEPTH = 1
DEC_BATCH = 1
DEC_SEQ = 32
PAST_LEN = 512

CHUNK = 64
HEAD_DIM = 64
MIX_WIDTH = D_MODEL
SB_HEADS = (MIX_WIDTH // 2) // HEAD_DIM
WIN_HEADS = (MIX_WIDTH // 2) // HEAD_DIM
WIN_KV_HEADS = 2
WIN_GROUP = WIN_HEADS // WIN_KV_HEADS
WINDOW = 128
Q_BLOCK = 128
SB_WIDTH = SB_HEADS * HEAD_DIM
WIN_WIDTH = WIN_HEADS * HEAD_DIM
WIN_KV_WIDTH = WIN_KV_HEADS * HEAD_DIM
SPLIT_SIZES = (SB_WIDTH, SB_WIDTH, SB_WIDTH, SB_WIDTH,
               WIN_WIDTH, WIN_KV_WIDTH, WIN_KV_WIDTH, WIN_WIDTH)
IN_WIDTH = sum(SPLIT_SIZES)
RMS_EPS = 1e-6

kernel_name = 'hybrid_stickbreak_swa_stream_step'

def rms_norm(x, g):
    xf = x.astype(jnp.float32)
    y = xf * lax.rsqrt(jnp.mean(xf * xf, axis=-1, keepdims=True) + RMS_EPS)
    return (y * g.astype(jnp.float32)).astype(x.dtype)

def alibi_slopes(n):
    return 2.0 ** (-8.0 * jnp.arange(1, n + 1, dtype=jnp.float32) / n)

def project(x, norm_g, w_in, q_norm_g, k_norm_g):
    B, T = x.shape[:2]
    z = rms_norm(x, norm_g) @ w_in
    offs = np.cumsum((0,) + SPLIT_SIZES)
    p = [z[..., int(offs[i]):int(offs[i + 1])] for i in range(len(SPLIT_SIZES))]
    sb_q = p[0].reshape(B, T, SB_HEADS, HEAD_DIM)
    sb_k = p[1].reshape(B, T, SB_HEADS, HEAD_DIM)
    sb_v = p[2].reshape(B, T, SB_HEADS, HEAD_DIM)
    win_q = rms_norm(p[4].reshape(B, T, WIN_HEADS, HEAD_DIM), q_norm_g)
    win_k = rms_norm(p[5].reshape(B, T, WIN_KV_HEADS, HEAD_DIM), k_norm_g)
    win_v = p[6].reshape(B, T, WIN_KV_HEADS, HEAD_DIM)
    return sb_q, sb_k, sb_v, p[3], win_q, win_k, win_v, p[7]

def combine(x, sb_o, sb_gate, win_o, win_gate, w_out):
    B, T = x.shape[:2]
    mixed = jnp.concatenate([sb_o.reshape(B, T, SB_WIDTH) * jax.nn.silu(sb_gate),
                             win_o.reshape(B, T, WIN_WIDTH) * jax.nn.silu(win_gate)], axis=-1)
    return x + mixed @ w_out

def stick_breaking(q, k, v, q_pos, k_pos):
    z = jnp.einsum('bqhd,bkhd->bhqk', q, k).astype(jnp.float32) * (HEAD_DIM ** -0.5)
    mask = k_pos[None, :] < q_pos[:, None]
    log_keep = jnp.where(mask, jax.nn.log_sigmoid(-z), 0.0)
    after = lax.cumsum(log_keep, axis=3, reverse=True) - log_keep
    w = jnp.where(mask, jnp.exp(jax.nn.log_sigmoid(z) + after), 0.0)
    return jnp.einsum('bhqk,bkhd->bqhd', w.astype(v.dtype), v)

def sb_prompt(q, k, v):
    B, S = q.shape[:2]
    nb = S // Q_BLOCK
    qb = q.reshape(B, nb, Q_BLOCK, SB_HEADS, HEAD_DIM).transpose(1, 0, 2, 3, 4)
    pos = jnp.arange(S)
    qpos = pos.reshape(nb, Q_BLOCK)
    out = lax.map(lambda a: stick_breaking(a[0], k, v, a[1], pos), (qb, qpos))
    return out.transpose(1, 0, 2, 3, 4).reshape(B, S, SB_HEADS, HEAD_DIM)

def sink_attention(q, k, v, keep, dist, slopes, sink):
    s = jnp.einsum('bnqhgd,bnkhd->bnhgqk', q, k).astype(jnp.float32) * (HEAD_DIM ** -0.5)
    s = s - slopes.reshape(WIN_KV_HEADS, WIN_GROUP)[:, :, None, None] * dist
    s = jnp.where(keep[None, :, None, None], s, -jnp.inf)
    sk = sink.astype(jnp.float32).reshape(WIN_KV_HEADS, WIN_GROUP)[:, :, None, None]
    m = jnp.maximum(jnp.max(s, axis=-1, keepdims=True), sk)
    p = jnp.exp(s - m)
    p = p / (jnp.sum(p, axis=-1, keepdims=True) + jnp.exp(sk - m))
    return jnp.einsum('bnhgqk,bnkhd->bnqhgd', p.astype(v.dtype), v)

def window_prompt(q, k, v, slopes, sink):
    B, S = q.shape[:2]
    nc = S // CHUNK
    nprev = WINDOW // CHUNK
    tk = WINDOW + CHUNK
    pad = ((0, 0), (WINDOW, 0), (0, 0), (0, 0))
    kp = jnp.pad(k, pad).reshape(B, nc + nprev, CHUNK, WIN_KV_HEADS, HEAD_DIM)
    vp = jnp.pad(v, pad).reshape(B, nc + nprev, CHUNK, WIN_KV_HEADS, HEAD_DIM)
    kb = jnp.concatenate([kp[:, i:i + nc] for i in range(nprev + 1)], axis=2)
    vb = jnp.concatenate([vp[:, i:i + nc] for i in range(nprev + 1)], axis=2)
    qc = q.reshape(B, nc, CHUNK, WIN_KV_HEADS, WIN_GROUP, HEAD_DIM)
    i = jnp.arange(CHUNK)
    j = jnp.arange(tk)
    dist = jnp.abs((j[None, :] - WINDOW) - i[:, None]).astype(jnp.float32)
    kpos = jnp.arange(nc)[:, None] * CHUNK - WINDOW + j[None, :]
    keep = jnp.broadcast_to((kpos >= 0)[:, None, :], (nc, CHUNK, tk))
    o = sink_attention(qc, kb, vb, keep, dist, slopes, sink)
    return o.reshape(B, S, WIN_HEADS, HEAD_DIM)

def window_sample(q, k_all, v_all, slopes, sink):
    B, T = q.shape[:2]
    tk = k_all.shape[1]
    tpos = (tk - T) + jnp.arange(T)
    spos = jnp.arange(tk)
    dist = jnp.abs(tpos[:, None] - spos[None, :]).astype(jnp.float32)
    keep = jnp.ones((1, T, tk), dtype=bool)
    qc = q.reshape(B, 1, T, WIN_KV_HEADS, WIN_GROUP, HEAD_DIM)
    o = sink_attention(qc, k_all[:, None], v_all[:, None], keep, dist, slopes, sink)
    return o.reshape(B, T, WIN_HEADS, HEAD_DIM)

def setup_inputs(seed: int = 0) -> dict:
    key = jax.random.key(seed)
    ks = jax.random.split(key, 13)
    f32 = jnp.float32
    return {
        'x_prompt': jax.random.normal(ks[0], (BATCH, SEQ, D_MODEL), f32),
        'x_sample': jax.random.normal(ks[1], (DEC_BATCH, DEC_SEQ, D_MODEL), f32),
        'cache_sb_k': jax.random.normal(ks[2], (DEPTH, DEC_BATCH, PAST_LEN, SB_HEADS, HEAD_DIM), f32),
        'cache_sb_v': jax.random.normal(ks[3], (DEPTH, DEC_BATCH, PAST_LEN, SB_HEADS, HEAD_DIM), f32),
        'cache_win_k': jax.random.normal(ks[4], (DEPTH, DEC_BATCH, WINDOW, WIN_KV_HEADS, HEAD_DIM), f32),
        'cache_win_v': jax.random.normal(ks[5], (DEPTH, DEC_BATCH, WINDOW, WIN_KV_HEADS, HEAD_DIM), f32),
        'norm_g': 1.0 + 0.02 * jax.random.normal(ks[6], (DEPTH, D_MODEL), f32),
        'w_in': jax.random.normal(ks[7], (DEPTH, D_MODEL, IN_WIDTH), f32) * D_MODEL ** -0.5,
        'q_norm_g': 1.0 + 0.02 * jax.random.normal(ks[8], (DEPTH, HEAD_DIM), f32),
        'k_norm_g': 1.0 + 0.02 * jax.random.normal(ks[9], (DEPTH, HEAD_DIM), f32),
        'attn_sink': 0.5 * jax.random.normal(ks[10], (DEPTH, WIN_HEADS), f32),
        'w_out': jax.random.normal(ks[11], (DEPTH, MIX_WIDTH, D_MODEL), f32) * MIX_WIDTH ** -0.5,
    }

def reference(x_prompt, x_sample, cache_sb_k, cache_sb_v, cache_win_k, cache_win_v,
              norm_g, w_in, q_norm_g, k_norm_g, attn_sink, w_out):
    slopes = alibi_slopes(WIN_HEADS)
    xp, xs = x_prompt, x_sample
    p_sbk, p_sbv, p_wk, p_wv = [], [], [], []
    s_sbk, s_sbv, s_wk, s_wv = [], [], [], []
    for l in range(DEPTH):
        sq, sk, sv, sg, wq, wk, wv, wg = project(xp, norm_g[l], w_in[l], q_norm_g[l], k_norm_g[l])
        sb_o = sb_prompt(sq, sk, sv)
        win_o = window_prompt(wq, wk, wv, slopes, attn_sink[l])
        xp = combine(xp, sb_o, sg, win_o, wg, w_out[l])
        p_sbk.append(sk)
        p_sbv.append(sv)
        p_wk.append(wk[:, -WINDOW:])
        p_wv.append(wv[:, -WINDOW:])

        sq, sk, sv, sg, wq, wk, wv, wg = project(xs, norm_g[l], w_in[l], q_norm_g[l], k_norm_g[l])
        past = cache_sb_k.shape[2]
        t_new = xs.shape[1]
        k_all = jnp.concatenate([cache_sb_k[l], sk], axis=1)
        v_all = jnp.concatenate([cache_sb_v[l], sv], axis=1)
        sb_o = stick_breaking(sq, k_all, v_all, past + jnp.arange(t_new), jnp.arange(past + t_new))
        wk_all = jnp.concatenate([cache_win_k[l], wk], axis=1)
        wv_all = jnp.concatenate([cache_win_v[l], wv], axis=1)
        win_o = window_sample(wq, wk_all, wv_all, slopes, attn_sink[l])
        xs = combine(xs, sb_o, sg, win_o, wg, w_out[l])
        s_sbk.append(sk)
        s_sbv.append(sv)
        s_wk.append(wk_all[:, -WINDOW:])
        s_wv.append(wv_all[:, -WINDOW:])

    return (xp, xs,
            jnp.stack(p_sbk), jnp.stack(p_sbv), jnp.stack(p_wk), jnp.stack(p_wv),
            jnp.stack(s_sbk), jnp.stack(s_sbv), jnp.stack(s_wk), jnp.stack(s_wv))


_drawn_inputs = setup_inputs


def setup_inputs(seed=0):
    import zlib

    import numpy as np

    out = dict(_drawn_inputs(seed))
    spreads = {}
    factors = {'norm_g': 2.708, 'q_norm_g': 8.0, 'attn_sink': 6.772}
    for name, (base, spread) in spreads.items():
        noise = np.random.default_rng([zlib.crc32(name.encode()), seed]).standard_normal(out[name].shape)
        drawn = base * np.exp(spread * noise) if base else spread * noise
        out[name] = __import__('jax').numpy.asarray(drawn.astype(out[name].dtype))
    for name, factor in factors.items():
        out[name] = (out[name] * factor).astype(out[name].dtype)
    return out
```

```python
from contextlib import ExitStack

import concourse.bass as bass
from concourse import mybir

F32 = mybir.dt.float32
F32R = mybir.dt.float32r
ACT = mybir.ActivationFunctionType
ALU = mybir.AluOpType
AX = mybir.AxisListType

P = 128
T, NS, D = 2048, 32, 1024
TT = T + NS
DT = D // P
HD, HEADS, KV = 64, 8, 2
PAIRS = HEADS // 2
GROUP = HEADS // KV
SB = 512
NSB = T // SB
QB = SB // P
PAST, WINDOW = 512, 128
EPS = 1e-6
MASKED = 1e30
SCALE = HD ** -0.5
SLOPE = [2.0 ** (-8.0 * (h + 1) / HEADS) for h in range(HEADS)]
COL_Q, COL_K, COL_V, COL_G, COL_WQ, COL_WK, COL_WV, COL_WG = 0, 512, 1024, 1536, 2048, 2560, 2688, 2816


def f32(ap):
    return ap.bitcast(F32)


class Shared:
    pass


def norm_stage(nc, s, ctx_x):
    with ExitStack() as ctx:
        sb = lambda name, shape, dt=F32: ctx.enter_context(nc.sbuf_tensor(name, shape, dt))
        sem = lambda name: ctx.enter_context(nc.semaphore(name))
        x = sb("x_rows", [P, 2, QB, D])
        xs_rows = sb("xs_rows", [NS, D])
        squares = sb("squares", [P, D])
        ssq = sb("ssq", [P, 2, QB])
        rstd = sb("rstd", [P, 2, QB])
        ssq_s = sb("ssq_s", [NS, 1])
        rstd_s = sb("rstd_s", [NS, 1])
        minus_half, eps_row = sb("minus_half", [P, QB]), sb("eps_row", [P, QB])
        grow = sb("grow", [DT, P])
        qkrow = sb("qkrow", [2, P])
        gcol = sb("gcol", [P, DT])
        xs_t = sb("xs_t", [P, DT, NS])
        ps = [ctx.enter_context(nc.psum_tensor(f"xt{i}", [P, SB], F32)) for i in range(DT)]
        x_in = [sem("x_in0"), sem("x_in1")]
        small_in, consts, squared, rstd_ready = sem("small_in"), sem("consts"), sem("squared"), sem("rstd_ready")
        scaled, transposed, hi_done, lo_done = sem("scaled"), sem("transposed"), sem("hi_done"), sem("lo_done")
        g_turned, g_ready, dist_abs = sem("g_turned"), sem("g_ready"), sem("dist_abs")
        rstd_step = sem("rstd_step")
        block = ctx.enter_context(nc.Block())
        x_sb = s.x_prompt.rearrange("(s j p) d -> s p j d", p=P, j=QB)

        @block.sync
        def _(sp):
            sp.dma_start(grow[:], s.norm_g.rearrange("o (a p) -> (o a) p", p=P)).then_inc(small_in, 16)
            for half in range(2):
                sp.dma_start(qkrow[0:1, half * HD:(half + 1) * HD], s.q_norm_g).then_inc(small_in, 16)
                sp.dma_start(qkrow[1:2, half * HD:(half + 1) * HD], s.k_norm_g).then_inc(small_in, 16)
            sp.dma_start(xs_rows[:], s.x_sample).then_inc(small_in, 16)
            with sp.Fori(0, NSB // 2) as i:
                for u in range(2):
                    sp.wait_ge(transposed, 2 * DT * i)
                    sp.dma_start(x[:, u], x_sb[2 * i + u]).then_inc(x_in[u], 16)

        @block.gpsimd
        def _(pool):
            pool.memset(s.ident[:], 0.0).then_inc(consts, 1)
            pool.memset(minus_half[:], -0.5).then_inc(consts, 1)
            pool.memset(eps_row[:], EPS)
            pool.memset(s.eps[:], EPS).then_inc(consts, 1)
            pool.memset(s.causal[:], 0.0).then_inc(consts, 1)
            pool.iota(s.dist[:, 0, 0:P], [[-1, P]], base=0, channel_multiplier=1,
                      allow_small_or_imprecise_dtypes=True).then_inc(consts, 1)
            pool.iota(s.dist[:, 0, P:2 * P], [[-1, P]], base=P, channel_multiplier=1,
                      allow_small_or_imprecise_dtypes=True).then_inc(consts, 1)
            pool.wait_ge(consts, 6)
            pool.affine_select(out=s.ident[:], in_=s.ident[:], compare_op=ALU.not_equal, fill=1.0, base=0,
                               pattern=[[-1, P]], channel_multiplier=1).then_inc(consts, 1)
            pool.affine_select(out=s.causal[:], in_=s.causal[:], compare_op=ALU.is_gt, fill=-MASKED, base=0,
                               pattern=[[-1, P]], channel_multiplier=1).then_inc(consts, 1)
            pool.wait_ge(squared, 1)
            pool.tensor_tensor(rstd_s[:], ssq_s[:], eps_row[0:NS, 0:1], ALU.add).then_inc(rstd_step, 1)
            pool.wait_ge(rstd_step, 1)
            pool.tensor_tensor(rstd_s[:], rstd_s[:], minus_half[0:NS, 0:1], ALU.pow).then_inc(rstd_ready, 1)
            with pool.Fori(0, NSB // 2) as i:
                for u in range(2):
                    pool.wait_ge(squared, 2 * QB * i + QB * (u + 1) + 1)
                    pool.wait_ge(scaled, 2 * QB * i)
                    pool.tensor_tensor(rstd[:, u], ssq[:, u], eps_row[:], ALU.add).then_inc(rstd_step, 1)
                    pool.wait_ge(rstd_step, 2 * i + u + 2)
                    pool.tensor_tensor(rstd[:, u], rstd[:, u], minus_half[:], ALU.pow).then_inc(rstd_ready, 1)

        @block.scalar
        def _(act):
            act.wait_ge(small_in, 6 * 16)
            act.activation(squares[0:NS, :], xs_rows[:], ACT.Square, scale=D ** -0.5, accum_out=ssq_s[:]).then_inc(squared, 1)
            act.wait_ge(consts, 6)
            act.activation(s.dist[:, 0, :], s.dist[:, 0, :], ACT.Abs).then_inc(dist_abs, 1)
            act.wait_ge(consts, 8)
            act.activation(s.causal_r[:], s.causal[:], ACT.Copy).then_inc(dist_abs, 1)
            act.activation(s.ident_r[:], s.ident[:], ACT.Copy).then_inc(dist_abs, 1)
            act.wait_ge(g_turned, 1)
            act.activation(gcol[:], ps[0][:, 0:DT], ACT.Copy).then_inc(g_ready, 1)
            act.wait_ge(g_turned, 2)
            act.activation(s.qk_gain[:, 0:1], ps[1][:, 0:1], ACT.Copy, scale=SCALE).then_inc(g_ready, 1)
            act.activation(s.qk_gain[:, 1:2], ps[1][:, 1:2], ACT.Copy).then_inc(g_ready, 1)
            act.wait_ge(g_ready, 3)
            with act.Fori(0, NSB // 2) as i:
                for u in range(2):
                    act.wait_ge(x_in[u], 16 * i + 16)
                    for j in range(QB):
                        act.wait_ge(squared, 2 * QB * i + QB * u + j + 1)
                        act.wait_ge(rstd_step, 2 * i + 1)
                        act.activation(squares[:], x[:, u, j, :], ACT.Square, scale=D ** -0.5,
                                       accum_out=ssq[:, u, j:j + 1]).then_inc(squared, 1)
                    for dt in range(DT):
                        act.wait_ge(transposed, 2 * DT * i + DT * u + dt + 1)
                        act.activation(s.XH[:, dt, bass.ds(SB * (2 * i + u), SB)], ps[dt][:], ACT.Copy,
                                       scale=gcol[:, dt:dt + 1]).then_inc(hi_done, 1)
            act.wait_ge(lo_done, NSB * DT + 1)
            act.activation(s.XH[:, :, T:TT], xs_t[:], ACT.Copy).then_inc(hi_done, 1)

        @block.vector
        def _(dve):
            dve.memset(s.ones_head[:], 0.0).then_inc(s.dist_ready, 1)
            dve.wait_ge(s.dist_ready, 1)
            for h in range(2):
                r = slice(h * HD, (h + 1) * HD)
                dve.memset(s.ones_head[r, r], 1.0).then_inc(s.dist_ready, 1)
            dve.wait_ge(dist_abs, 1)
            dve.memset(s.dist[0:HD, 0, HD:P], MASKED).then_inc(s.dist_ready, 1)
            dve.memset(s.dist[HD:P, 0, P:P + HD], MASKED).then_inc(s.dist_ready, 1)
            dve.wait_ge(s.dist_ready, 5)
            dve.tensor_copy(s.dist[:, 1, P:2 * P], s.dist[:, 0, 0:P]).then_inc(s.dist_ready, 1)
            dve.tensor_copy(s.dist[:, 1, 0:P], s.dist[:, 0, P:2 * P]).then_inc(s.dist_ready, 1)
            dve.tensor_copy(s.dist[:, 2, 0:P], s.dist[:, 0, 0:P]).then_inc(s.dist_ready, 1)
            dve.memset(s.dist[:, 2, P:2 * P], MASKED).then_inc(s.dist_ready, 1)
            dve.wait_ge(rstd_ready, 1)
            dve.tensor_scalar(xs_rows[:], xs_rows[:], rstd_s[:], None, ALU.mult).then_inc(scaled, 1)
            dve.wait_ge(g_ready, 3)
            with dve.Fori(0, NSB // 2) as i:
                for u in range(2):
                    dve.wait_ge(rstd_ready, 2 * i + u + 2)
                    for j in range(QB):
                        dve.tensor_scalar(x[:, u, j, :], x[:, u, j, :], rstd[:, u, j:j + 1], None,
                                          ALU.mult).then_inc(scaled, 1)
                    for dt in range(DT):
                        dve.wait_ge(hi_done, 2 * DT * i + DT * u + dt + 1)
                        dve.scalar_tensor_tensor(out=s.XL[:, dt, bass.ds(SB * (2 * i + u), SB)], in0=ps[dt][:],
                                                 scalar=gcol[:, dt:dt + 1],
                                                 in1=f32(s.XH[:, dt, bass.ds(SB * (2 * i + u), SB)]),
                                                 op0=ALU.mult, op1=ALU.subtract).then_inc(lo_done, 1)
            dve.wait_ge(transposed, NSB * DT + 1)
            dve.tensor_tensor(xs_t[:], ps[0][:, 0:DT * NS].rearrange("p (a t) -> p a t", a=DT),
                              gcol[:].unsqueeze(2).to_broadcast([P, DT, NS]), ALU.mult).then_inc(lo_done, 1)
            dve.wait_ge(hi_done, NSB * DT + 1)
            dve.tensor_tensor(s.XL[:, :, T:TT], xs_t[:], f32(s.XH[:, :, T:TT]), ALU.subtract).then_inc(lo_done, 1)

        @block.tensor
        def _(pe):
            pe.wait_ge(consts, 7)
            pe.wait_ge(small_in, 6 * 16)
            pe.transpose(ps[0][:, 0:DT], grow[:], s.ident[0:DT, 0:DT]).then_inc(g_turned, 1)
            pe.transpose(ps[1][:, 0:2], qkrow[:], s.ident[0:2, 0:2]).then_inc(g_turned, 1)
            pe.wait_ge(g_ready, 3)
            with pe.Fori(0, NSB // 2) as i:
                for u in range(2):
                    pe.wait_ge(scaled, 2 * QB * i + QB * (u + 1) + 1)
                    for dt in range(DT):
                        pe.wait_ge(lo_done, 2 * DT * i + (dt + 1 if u else 0))
                        for j in range(QB):
                            last = pe.transpose(ps[dt][:, j * P:(j + 1) * P], x[:, u, j, dt * P:(dt + 1) * P],
                                                s.ident[:])
                        last.then_inc(transposed, 1)
            pe.wait_ge(lo_done, NSB * DT)
            for dt in range(DT):
                last = pe.transpose(ps[0][:, dt * NS:(dt + 1) * NS], xs_rows[:, dt * P:(dt + 1) * P],
                                    s.ident[0:NS, 0:NS])
            last.then_inc(transposed, 1)


def weight_parts(nc, ctx, tag, sets):
    w = Shared()
    w.raw = ctx.enter_context(nc.sbuf_tensor(f"{tag}_w_raw", [P, DT, P], F32))
    w.hi = [ctx.enter_context(nc.sbuf_tensor(f"{tag}_w_hi{n}", [P, DT, P], F32R)) for n in range(sets)]
    w.lo = [ctx.enter_context(nc.sbuf_tensor(f"{tag}_w_lo{n}", [P, DT, P], F32R)) for n in range(sets)]
    w.raw_in, w.hi_ready, w.lo_ready = (
        ctx.enter_context(nc.semaphore(f"{tag}_w_{n}")) for n in ("raw_in", "hi_ready", "lo_ready"))
    return w


def load_weights(sp, s, w, c, col):
    sp.wait_ge(w.lo_ready, c)
    sp.dma_start(w.raw[:], s.w_in[:, :, bass.ds(col, P)]).then_inc(w.raw_in, 16)


def split_weights_hi(act, w, c, n, group_ready, groups):
    act.wait_ge(w.raw_in, 16 * c + 16)
    act.wait_ge(group_ready, groups)
    act.activation(w.hi[n][:], w.raw[:], ACT.Copy).then_inc(w.hi_ready, 1)


def split_weights_lo(pool, w, c, n):
    pool.wait_ge(w.hi_ready, c + 1)
    pool.tensor_tensor(w.lo[n][:], w.raw[:], f32(w.hi[n][:]), ALU.subtract).then_inc(w.lo_ready, 1)


def project(pe, s, w, n, out, t0, cols):
    for dt in range(DT):
        xh, xl = s.XH[:, dt, t0:t0 + cols], s.XL[:, dt, t0:t0 + cols]
        pe.matmul(out, w.hi[n][:, dt, :], xh, start=(dt == 0), stop=False)
        pe.matmul(out, w.hi[n][:, dt, :], xl, start=False, stop=False)
        last = pe.matmul(out, w.lo[n][:, dt, :], xh, start=False, stop=(dt == DT - 1))
    return last


GROUPS = [(SB * t, SB) for t in range(NSB)] + [(T, NS)]
NG = len(GROUPS)
BANK = [0, 1, 0, 1, 2]
AHEAD = 2


def wait_bank(pe, group_free, first, t):
    back = {0: 3, 1: 3, 2: 2, 3: 2, 4: NG}[t]
    pe.wait_ge(group_free, first + t - back + 1 + AHEAD)


def window_project_stage(nc, s):
    with ExitStack() as ctx:
        sb = lambda name, shape, dt=F32: ctx.enter_context(nc.sbuf_tensor(name, shape, dt))
        sem = lambda name: ctx.enter_context(nc.semaphore(name))
        w = weight_parts(nc, ctx, "a", 2)
        sq = sb("a_sq", [P, 2, SB])
        raw = sb("a_raw", [P, 2, SB])
        root = sb("a_root", [P, SB])
        inv = sb("a_inv", [P, SB])
        nst = sb("a_nst", [P, 2, SB])
        vrow = sb("a_vrow", [P, QB, P])
        vpart = sb("a_vpart", [P, QB, KV, P], F32R)
        bank = [ctx.enter_context(nc.psum_tensor(f"a_ps{i}", [P, SB], F32)) for i in range(5)]
        sums = bank[3:5]
        group_ready, group_free = sem("a_group_ready"), sem("a_group_free")
        squared, summed, rooted, inverted = sem("a_squared"), sem("a_summed"), sem("a_rooted"), sem("a_inverted")
        normed, stored = sem("a_normed"), [sem("a_stored0"), sem("a_stored1")]
        v_raw, v_turned, v_rows, v_hi, v_lo, v_stored = (
            sem("a_" + n) for n in ("v_raw", "v_turned", "v_rows", "v_hi", "v_lo", "v_stored"))
        block = ctx.enter_context(nc.Block())
        QC = 4

        @block.sync
        def _(sp):
            def chunk(c, u):
                load_weights(sp, s, w, c + 1, COL_WQ + P * (c + 1))
                for t, (t0, n) in enumerate(GROUPS):
                    g = (NG * u + t) % 2
                    sp.wait_ge(normed, NG * c + t + 1 + AHEAD)
                    sp.dma_start(s.normT[c, :, t0:t0 + n], nst[:, g, 0:n]).then_inc(stored[g], 16)

            load_weights(sp, s, w, 0, COL_WQ)
            with sp.Fori(0, QC // 2) as i:
                for u in range(2):
                    chunk(2 * i + u, u)
            chunk(QC, 0)
            for t, (t0, n) in enumerate(GROUPS):
                sp.wait_ge(v_rows, t + 1)
                if t < NSB:
                    sp.dma_start(s.win_v_rows[t0:t0 + n, :].rearrange("(j p) c -> p j c", p=P),
                                 vrow[:]).then_inc(v_stored, 16)
                    sp.wait_ge(v_lo, t + 1)
                    sp.dma_start(s.win_v_parts[t], f32(vpart[:].rearrange("p j g c -> p (j g c)"))).then_inc(v_stored, 16)
                else:
                    sp.dma_start(s.win_v_rows[t0:t0 + n, :], vrow[0:NS, 0, :]).then_inc(v_stored, 16)
            sp.wait_ge(v_stored, (2 * NSB + 1) * 16)
            sp.wait_ge(stored[0], 13 * 16)
            sp.wait_ge(stored[1], 12 * 16)

        @block.gpsimd
        def _(pool):
            with pool.Fori(0, QC // 2 + 1) as i:
                for u in range(2):
                    split_weights_lo(pool, w, 2 * i + u, u)
            for t in range(NSB):
                pool.wait_ge(v_hi, t + 1)
                pool.wait_ge(v_rows, t + 1)
                pool.tensor_tensor(vpart[:, :, :, HD:P], vrow[:].rearrange("p j (g c) -> p j g c", g=KV),
                                   f32(vpart[:, :, :, 0:HD]), ALU.subtract).then_inc(v_lo, 1)

        @block.scalar
        def _(act):
            act.sem_inc(group_free, AHEAD)
            act.sem_inc(rooted, AHEAD)

            def roots(m, n, g):
                act.wait_ge(summed, m + 1)
                act.wait_ge(inverted, m)
                act.activation(root[:, 0:n], sums[g][:, 0:n], ACT.Sqrt, scale=1.0 / HD,
                               bias=s.eps[:]).then_inc(rooted, 1)

            def chunk(c, u):
                first = NG * c
                for t, (t0, n) in enumerate(GROUPS):
                    m, g = first + t, (NG * u + t) % 2
                    act.wait_ge(group_ready, m + 1)
                    act.wait_ge(normed, m - 1 + AHEAD)
                    act.wait_ge(rooted, m - 1 + AHEAD)
                    act.activation(sq[:, g, 0:n], bank[BANK[t]][:, 0:n], ACT.Square).then_inc(squared, 1)
                    act.activation(raw[:, g, 0:n], bank[BANK[t]][:, 0:n], ACT.Copy).then_inc(group_free, 1)
                    if t == 1:
                        split_weights_hi(act, w, c + 1, (u + 1) % 2, group_ready, NG * c)
                    if t:
                        roots(m - 1, GROUPS[t - 1][1], 1 - g)
                roots(first + NG - 1, NS, (NG * u + NG - 1) % 2)

            split_weights_hi(act, w, 0, 0, group_ready, 0)
            with act.Fori(0, QC // 2) as i:
                for u in range(2):
                    chunk(2 * i + u, u)
            chunk(QC, 0)
            for t, (t0, n) in enumerate(GROUPS):
                act.wait_ge(group_ready, NG * (QC + 1) + t + 1)
                act.wait_ge(normed, NG * (QC + 1) + AHEAD)
                act.wait_ge(v_turned, t)
                act.activation(raw[:, 0, 0:n], bank[BANK[t]][:, 0:n], ACT.Copy).then_inc(v_raw, 1)
                act.wait_ge(v_turned, t + 1)
                act.wait_ge(v_stored, 32 * t)
                if t < NSB:
                    act.activation(vrow[:].rearrange("p j c -> p (j c)"), sums[0][:], ACT.Copy).then_inc(v_rows, 1)
                    act.activation(vpart[:, :, :, 0:HD], sums[0][:].rearrange("p (j g c) -> p j g c", g=KV, c=HD),
                                   ACT.Copy).then_inc(v_hi, 1)
                else:
                    act.activation(vrow[0:NS, 0, :], sums[0][0:NS, 0:P], ACT.Copy).then_inc(v_rows, 1)

        @block.vector
        def _(dve):
            dve.sem_inc(normed, AHEAD)

            def chunk(c, u, stores, gain):
                for t, (t0, n) in enumerate(GROUPS):
                    m, g = NG * c + t, (NG * u + t) % 2
                    dve.wait_ge(rooted, m + 1 + AHEAD)
                    dve.wait_ge(normed, m + AHEAD)
                    dve.reciprocal(inv[:, 0:n], root[:, 0:n]).then_inc(inverted, 1)
                    dve.wait_ge(inverted, m + 1)
                    dve.wait_ge(stored[g], 16 * (stores + (NG * u + t) // 2))
                    dve.wait_ge(group_free, m + 1 + AHEAD)
                    dve.scalar_tensor_tensor(out=nst[:, g, 0:n], in0=raw[:, g, 0:n], scalar=gain,
                                             in1=inv[:, 0:n], op0=ALU.mult, op1=ALU.mult).then_inc(normed, 1)

            with dve.Fori(0, QC // 2) as i:
                for u in range(2):
                    chunk(2 * i + u, u, NG * i, s.qk_gain[:, 0:1])
            chunk(QC, 0, NG * QC // 2, s.qk_gain[:, 1:2])

        @block.tensor
        def _(pe):
            def sum_squares(m, n, g):
                pe.wait_ge(squared, m + 1)
                pe.wait_ge(rooted, m - 1 + AHEAD)
                pe.matmul(sums[g][:, 0:n], s.ones_head[:], sq[:, g, 0:n], start=True, stop=True).then_inc(summed, 1)

            def chunk(c, u):
                first = NG * c
                pe.wait_ge(w.lo_ready, c + 1)
                for t, (t0, n) in enumerate(GROUPS):
                    wait_bank(pe, group_free, first, t)
                    project(pe, s, w, u % 2, bank[BANK[t]][:, 0:n], t0, n).then_inc(group_ready, 1)
                    if t:
                        sum_squares(first + t - 1, GROUPS[t - 1][1], (NG * u + t - 1) % 2)
                sum_squares(first + NG - 1, NS, (NG * u + NG - 1) % 2)

            with pe.Fori(0, QC // 2) as i:
                for u in range(2):
                    chunk(2 * i + u, u)
            chunk(QC, 0)
            first = NG * (QC + 1)
            pe.wait_ge(w.lo_ready, QC + 2)

            def turn_v(t, n):
                pe.wait_ge(v_raw, t + 1)
                pe.wait_ge(rooted, first + AHEAD)
                pe.wait_ge(v_rows, t)
                pe.wait_ge(v_hi, t)
                for j in range(max(1, n // P)):
                    rows = min(n, P)
                    last = pe.transpose(sums[0][0:rows, j * P:(j + 1) * P], raw[:, 0, j * P:j * P + rows], s.ident[:])
                last.then_inc(v_turned, 1)

            for t, (t0, n) in enumerate(GROUPS):
                if t < 2:
                    wait_bank(pe, group_free, first, t)
                elif t < NSB:
                    pe.wait_ge(v_raw, t - 1)
                project(pe, s, w, 1, bank[BANK[t]][:, 0:n], t0, n).then_inc(group_ready, 1)
                if t:
                    turn_v(t - 1, GROUPS[t - 1][1])
            turn_v(NG - 1, NS)


def pair_project_stage(nc, s):
    with ExitStack() as ctx:
        sb = lambda name, shape, dt=F32: ctx.enter_context(nc.sbuf_tensor(name, shape, dt))
        sem = lambda name: ctx.enter_context(nc.semaphore(name))
        K, V, Q, G, WG = range(5)
        SETS = [0, 1, 2, 0, 1]
        COLS = [COL_K, COL_V, COL_Q, COL_G, COL_WG]
        SLOTS, STEPS = 5 * NG, 2 * QB
        w = weight_parts(nc, ctx, "b", 3)
        raw = sb("b_raw", [P, 2, SB])
        raw_s = sb("b_raw_s", [P, NS])
        rows = sb("b_rows", [P, QB, P])
        kpart = sb("b_kpart", [P, 2, SB], F32R)
        vpart = sb("b_vpart", [P, 2, QB, P], F32R)
        qraw = sb("b_qraw", [P, HEADS, P])
        qpart = sb("b_qpart", [P, HEADS, P], F32R)
        kraw = sb("b_kraw", [P, KV, P])
        khi = sb("b_khi", [P, KV, 2, P], F32R)
        klo = sb("b_klo", [P, KV, 2, P], F32R)
        vwin = sb("b_vwin", [P, 2, KV, P], F32R)
        prob = sb("b_prob", [P, GROUP, 2 * P])
        pt_hi = [sb(f"b_pt_hi{n}", [P, GROUP * P], F32R) for n in range(2)]
        pt_lo = [sb(f"b_pt_lo{n}", [P, GROUP * P], F32R) for n in range(2)]
        o_sum = sb("b_o_sum", [P, GROUP * P])
        sink = sb("b_sink", [P, HEADS])
        neg_sink = sb("b_neg_sink", [P, HEADS])
        neg_max, shift, sink_in, sink_e, total, denom, inv = (
            sb("b_" + n, [P, GROUP]) for n in ("neg_max", "shift", "sink_in", "sink_e", "total", "denom", "inv"))
        bank = [ctx.enter_context(nc.psum_tensor(f"b_ps{i}", [P, SB], F32)) for i in range(3)]
        turned_ps = ctx.enter_context(nc.psum_tensor("b_turned", [P, SB], F32))
        score = ctx.enter_context(nc.psum_tensor("b_score", [P, GROUP, 2 * P], F32))
        pt_ps = ctx.enter_context(nc.psum_tensor("b_pt", [P, GROUP * P], F32))
        o_ps = ctx.enter_context(nc.psum_tensor("b_o", [P, GROUP * P], F32))
        group_ready, group_out, k_lo_done = sem("b_group_ready"), sem("b_group_out"), sem("b_k_lo_done")
        k_hi_ready = sem("b_k_hi_ready")
        turned, k_rows, v_rows, v_hi, v_lo = (sem("b_" + n) for n in ("turned", "k_rows", "v_rows", "v_hi", "v_lo"))
        raw_stored, raw_s_stored = [sem("b_raw_stored0"), sem("b_raw_stored1")], sem("b_raw_s_stored")
        rows_stored, kpart_stored, vpart_stored = sem("b_rows_stored"), sem("b_kpart_stored"), sem("b_vpart_stored")
        sinks_in, block_in, v_block_in = sem("b_sinks_in"), sem("b_block_in"), sem("b_v_block_in")
        q_hi, q_ready, k_hi, k_ready, start_done = (
            sem("b_" + n) for n in ("q_hi", "q_ready", "k_hi", "k_ready", "start_done"))
        scored, biased, shifted, exped, normed = (
            sem("b_" + n) for n in ("scored", "biased", "shifted", "exped", "normed"))
        soft_step, sink_ready = sem("b_soft_step"), sem("b_sink_ready")
        probs_turned, pt_hi_ready, pt_lo_ready, mixed = (
            sem("b_" + n) for n in ("probs_turned", "pt_hi_ready", "pt_lo_ready", "mixed"))
        o_lo_out, o_ready, o_stored = sem("b_o_lo_out"), sem("b_o_ready"), sem("b_o_stored")
        block = ctx.enter_context(nc.Block())

        def buffer_free(eng, i, u, t):
            if t == NG - 1:
                if u == V:
                    eng.wait_ge(turned, 10 * i + NG)
                if u == Q:
                    eng.wait_ge(turned, 10 * i + 2 * NG)
                eng.wait_ge(raw_s_stored, 16 * (4 * i + {K: 0, V: 1, Q: 1, G: 2, WG: 3}[u]))
            elif 5 * u + t in (0, 1):
                eng.wait_ge(raw_stored[t], 16 * 6 * i)
            elif 5 * u + t <= 5 * Q + 1:
                back = {(K, 2): 1, (K, 3): 2, (V, 0): 3, (V, 1): 4, (V, 2): 6, (V, 3): 7, (Q, 0): 8, (Q, 1): 9}
                eng.wait_ge(turned, 10 * i + back[u, t])
            else:
                eng.wait_ge(raw_stored[t % 2], 16 * (6 * i + 2 * (u - Q) + t // 2))

        def turned_slot(n):
            return (divmod(n - 1, NG)) if 1 <= n <= 2 * NG else None

        @block.sync
        def _(sp):
            sp.dma_start(sink[:], s.attn_sink.to_broadcast([P, HEADS])).then_inc(sinks_in, 16)
            load_weights(sp, s, w, 0, COL_K)

            def load_block(b, i, j):
                sp.wait_ge(q_ready, b)
                sp.wait_ge(k_ready, b)
                for half in range(2):
                    r = slice(half * HD, (half + 1) * HD)
                    sp.dma_start(qraw[r], s.normT_q[:, :, bass.ds(P * b, P)]).then_inc(block_in, 16)
                    sp.dma_start(kraw[r], s.normT_k[:, :, bass.ds(P * b, P)]).then_inc(block_in, 16)

            def load_v_block(b, i, j):
                sp.wait_ge(mixed, 4 * b)
                sp.dma_start(f32(vwin[:, j % 2]).rearrange("p g c -> p (g c)"),
                             s.win_v_parts[i, :, j * KV * P:(j + 1) * KV * P]).then_inc(v_block_in, 16)

            with sp.Fori(0, PAIRS) as i:
                load_block(QB * i, i, 0)
                load_v_block(QB * i, i, 0)
                for n in range(SLOTS):
                    u, t = divmod(n, NG)
                    t0, cols = GROUPS[t]
                    c = 5 * i + u
                    if t == 0:
                        load_weights(sp, s, w, c + 1, COLS[(u + 1) % 5] + P * (i + (u == 4)))
                    if n % 6 == 3 and n < 21:
                        load_block(QB * i + n // 6 + 1, i, n // 6 + 1)
                    if u in (Q, G, WG):
                        sp.wait_ge(group_out, NG * c + t + 1 + AHEAD)
                        if u == Q:
                            out = s.qT[t, i] if t < NSB else s.qT_sample[i]
                        else:
                            out = s.gateT[i + (PAIRS if u == WG else 0), :, t0:t0 + cols]
                        if t < NSB:
                            sp.dma_start(out, raw[:, t % 2, :]).then_inc(raw_stored[t % 2], 16)
                        else:
                            sp.dma_start(out, raw_s[:]).then_inc(raw_s_stored, 16)
                    if u == K and t == NG - 1:
                        sp.wait_ge(group_out, NG * c + t + 1 + AHEAD)
                        sp.dma_start(s.kT_sample[i], raw_s[:]).then_inc(raw_s_stored, 16)
                    parts = sp.snap(sp.to_reg(4 * i + t + 1)) if n == 1 else 4 * i + t + 1
                    if n == 1:
                        sp.wait_ge(k_rows, NG * i + 1)
                    if u == K and t < NSB:
                        sp.wait_ge(k_lo_done, parts)
                        sp.dma_start(s.k_parts[t, bass.ds(2 * i, 2)].rearrange("h p c -> p h c"),
                                     f32(kpart[:])).then_inc(kpart_stored, 16)
                    if turned_slot(n):
                        x, xt = turned_slot(n)
                        if n > 1:
                            sp.wait_ge(v_rows if x == V else k_rows, NG * i + xt + 1)
                        big, small = (s.sb_v_rows, s.sb_v_sample) if x == V else (s.sb_k_rows, s.sb_k_sample)
                        if xt < NSB:
                            sp.dma_start(big[xt, :, :, bass.ds(P * i, P)], rows[:]).then_inc(rows_stored, 16)
                        else:
                            sp.dma_start(small[:, bass.ds(P * i, P)], rows[0:NS, 0, :]).then_inc(rows_stored, 16)
                        if x == V and xt < NSB:
                            sp.wait_ge(v_lo, 4 * i + xt + 1)
                            sp.dma_start(s.v_parts[xt, bass.ds(2 * i, 2)].rearrange("h p c -> p h c"),
                                         f32(vpart[:]).rearrange("p h j c -> p h (j c)")).then_inc(vpart_stored, 16)
                    if (n >= 4 and (n - 4) % 3 == 0) or n == SLOTS - 1:
                        st = 7 if n == SLOTS - 1 else (n - 4) // 3
                        j, g = divmod(st, KV)
                        sp.wait_ge(o_ready, STEPS * i + st + 1)
                        sp.dma_start(s.oT_win[g, :, :, bass.ds(P * (QB * i + j), P)],
                                     o_sum[0:HD].rearrange("p (h t) -> p h t", h=GROUP)).then_inc(o_stored, 16)
                        if g == 1 and j < QB - 1:
                            load_v_block(QB * i + j + 1, i, j + 1)
            for q, count in ((raw_stored[0], 6 * PAIRS), (raw_stored[1], 6 * PAIRS), (raw_s_stored, 4 * PAIRS),
                             (rows_stored, 10 * PAIRS), (kpart_stored, 4 * PAIRS), (vpart_stored, 4 * PAIRS),
                             (o_stored, STEPS * PAIRS)):
                sp.wait_ge(q, 16 * count)

        @block.gpsimd
        def _(pool):
            def k_lo_block(b, j):
                pool.wait_ge(k_hi, b + 1)
                pool.tensor_tensor(klo[:, :, j % 2, :], kraw[:], f32(khi[:, :, j % 2, :]),
                                   ALU.subtract).then_inc(k_ready, 1)

            split_weights_lo(pool, w, 0, 0)
            pool.wait_ge(start_done, 1)
            with pool.Fori(0, PAIRS) as i:
                k_lo_block(QB * i, 0)
                for n in range(SLOTS):
                    u, t = divmod(n, NG)
                    if t == 1:
                        split_weights_lo(pool, w, 5 * i + u + 1, SETS[(u + 1) % 5])
                    if turned_slot(n) and turned_slot(n)[0] == V and turned_slot(n)[1] < NSB:
                        xt = turned_slot(n)[1]
                        pool.wait_ge(v_hi, 4 * i + xt + 1)
                        pool.tensor_tensor(vpart[:, :, :, HD:P], rows[:].rearrange("p j (h c) -> p h j c", h=2),
                                           f32(vpart[:, :, :, 0:HD]), ALU.subtract).then_inc(v_lo, 1)
                    if n % 3 == 1 and n < 24:
                        st = n // 3
                        if st % 2 == 1 and st < STEPS - 1:
                            k_lo_block(QB * i + st // 2 + 1, st // 2 + 1)
                        pool.wait_ge(soft_step, 6 * (STEPS * i + st) + 6)
                        pool.tensor_tensor(prob[:], prob[:], inv[:].unsqueeze(2).to_broadcast([P, GROUP, 2 * P]),
                                           ALU.mult).then_inc(normed, 1)

        @block.scalar
        def _(act):
            def split_block(b, j):
                act.wait_ge(block_in, 64 * (b + 1))
                act.wait_ge(scored, 2 * b)
                act.activation(qpart[:], qraw[:], ACT.Copy).then_inc(q_hi, 1)
                act.activation(khi[:, :, j % 2, :], kraw[:], ACT.Copy).then_inc(k_hi, 1)

            def pt_hi_copy(i, st, slot):
                act.wait_ge(probs_turned, 2 * (STEPS * i + st) + slot + 1)
                act.wait_ge(mixed, 2 * (STEPS * i + st))
                act.activation(pt_hi[slot][:], pt_ps[:], ACT.Copy).then_inc(pt_hi_ready, 1)

            def o_copy(i, st):
                act.wait_ge(mixed, 2 * (STEPS * i + st) + 2)
                act.wait_ge(o_stored, 16 * (STEPS * i + st))
                act.activation(o_sum[HD:P, :], o_ps[HD:P, :], ACT.Copy).then_inc(o_lo_out, 1)

            act.sem_inc(group_out, AHEAD)
            split_weights_hi(act, w, 0, 0, group_ready, 0)
            act.wait_ge(start_done, 1)
            with act.Fori(0, PAIRS) as i:
                split_block(QB * i, 0)
                for n in range(SLOTS):
                    u, t = divmod(n, NG)
                    t0, cols = GROUPS[t]
                    m = NG * (5 * i + u) + t
                    ps = bank[BANK[t]]
                    act.wait_ge(group_ready, m + 1)
                    buffer_free(act, i, u, t)
                    out = raw[:, t % 2, :] if t < NSB else raw_s[:]
                    last = act.activation(out, ps[:, 0:cols], ACT.Copy)
                    if u == K and t < NSB:
                        act.wait_ge(kpart_stored, 16 * (4 * i + t))
                        act.activation(kpart[0:HD, 0, :], ps[0:HD, :], ACT.Copy).then_inc(k_hi_ready, 1)
                        last = act.activation(kpart[0:HD, 1, :], ps[HD:P, :], ACT.Copy)
                    last.then_inc(group_out, 1)
                    if t == 1:
                        split_weights_hi(act, w, 5 * i + u + 1, SETS[(u + 1) % 5], group_ready, NG * (5 * i + u))
                    if turned_slot(n) and turned_slot(n)[0] == V:
                        xt = turned_slot(n)[1]
                        act.wait_ge(turned, 10 * i + NG + xt + 1)
                        act.wait_ge(rows_stored, 16 * (10 * i + NG + xt))
                        if xt < NSB:
                            act.wait_ge(v_lo, 4 * i + xt)
                            act.activation(rows[:].rearrange("p j c -> p (j c)"), turned_ps[:], ACT.Copy)\
                               .then_inc(v_rows, 1)
                            act.wait_ge(vpart_stored, 16 * (4 * i + xt))
                            act.activation(vpart[:, :, :, 0:HD],
                                           turned_ps[:].rearrange("p (j h c) -> p h j c", h=2, c=HD),
                                           ACT.Copy).then_inc(v_hi, 1)
                        else:
                            act.wait_ge(v_lo, 4 * i + NSB)
                            act.activation(rows[0:NS, 0, :], turned_ps[0:NS, 0:P], ACT.Copy).then_inc(v_rows, 1)
                    if n % 3 == 1 and n < 24:
                        st = n // 3
                        if st:
                            o_copy(i, st - 1)
                        act.wait_ge(shifted, STEPS * i + st + 1)
                        for h in range(GROUP):
                            act.activation(prob[:, h, :], prob[:, h, :], ACT.Exp, bias=shift[:, h:h + 1],
                                           accum_out=total[:, h:h + 1]).then_inc(exped, 1)
                        act.activation(sink_e[:], sink_in[:], ACT.Exp).then_inc(exped, 1)
                        if st % 2 == 1 and st < STEPS - 1:
                            split_block(QB * i + st // 2 + 1, st // 2 + 1)
                    if n % 3 == 2:
                        pt_hi_copy(i, n // 3, 0)
                    if n % 3 == 0 and n:
                        pt_hi_copy(i, n // 3 - 1, 1)
                    if n == SLOTS - 1:
                        o_copy(i, STEPS - 1)

        @block.vector
        def _(dve):
            def q_lo_block(b):
                dve.wait_ge(q_hi, b + 1)
                dve.tensor_tensor(qpart[HD:P], qraw[HD:P], f32(qpart[HD:P]), ALU.subtract).then_inc(q_ready, 1)

            def pt_lo_copy(i, st, slot):
                dve.wait_ge(pt_hi_ready, 2 * (STEPS * i + st) + slot + 1)
                dve.tensor_tensor(pt_lo[slot][:], pt_ps[:], f32(pt_hi[slot][:]), ALU.subtract).then_inc(pt_lo_ready, 1)

            def o_add(i, st):
                dve.wait_ge(o_lo_out, STEPS * i + st + 1)
                dve.tensor_tensor(o_sum[0:HD, :], o_ps[0:HD, :], o_sum[HD:P, :], ALU.add).then_inc(o_ready, 1)

            dve.memset(f32(khi[:, :, 1, :]), 0.0)
            dve.memset(f32(klo[:, :, 1, :]), 0.0)
            dve.memset(f32(vwin[:, 1]), 0.0).then_inc(start_done, 1)
            dve.wait_ge(sinks_in, 16)
            dve.tensor_scalar(neg_sink[:], sink[:], -1.0, None, ALU.mult).then_inc(sink_ready, 1)
            dve.wait_ge(sink_ready, 1)
            with dve.Fori(0, PAIRS) as i:
                q_lo_block(QB * i)
                for n in range(SLOTS):
                    u, t = divmod(n, NG)
                    if u == K and t < NSB:
                        for h in range(2):
                            if h == 0:
                                dve.wait_ge(k_hi_ready, 4 * i + t + 1)
                            else:
                                dve.wait_ge(group_out, NG * (5 * i + u) + t + 1 + AHEAD)
                            last = dve.tensor_tensor(kpart[HD:P, h, :], bank[BANK[t]][h * HD:(h + 1) * HD, :],
                                                     f32(kpart[0:HD, h, :]), ALU.subtract)
                        last.then_inc(k_lo_done, 1)
                    if turned_slot(n) and turned_slot(n)[0] == K:
                        xt = turned_slot(n)[1]
                        dve.wait_ge(turned, 10 * i + xt + 1)
                        dve.wait_ge(rows_stored, 16 * (10 * i + xt))
                        if xt < NSB:
                            if xt == 0:
                                dve.wait_ge(v_lo, 4 * i)
                            dve.tensor_copy(rows[:].rearrange("p j c -> p (j c)"), turned_ps[:]).then_inc(k_rows, 1)
                        else:
                            dve.tensor_copy(rows[0:NS, 0, :], turned_ps[0:NS, 0:P]).then_inc(k_rows, 1)
                    if n % 3 == 2:
                        pt_lo_copy(i, n // 3, 0)
                    if n % 3 == 0 and n:
                        pt_lo_copy(i, n // 3 - 1, 1)
                    if n % 3 == 1 and n > 3 and n < 24:
                        o_add(i, n // 3 - 1)
                    if n % 3 == 0 and n < 24:
                        st = n // 3
                        j, g = divmod(st, KV)
                        e = 6 * (STEPS * i + st)
                        heads = slice(GROUP * g, GROUP * (g + 1))
                        dve.wait_ge(scored, STEPS * i + st + 1)
                        dve.wait_ge(probs_turned, 2 * (STEPS * i + st))
                        table = 2 if j == 0 else j % 2
                        for h in range(GROUP):
                            last = dve.scalar_tensor_tensor(out=prob[:, h, :], in0=s.dist[:, table, :],
                                                            scalar=-SLOPE[GROUP * g + h], in1=score[:, h, :],
                                                            op0=ALU.mult, op1=ALU.add)
                        last.then_inc(soft_step, 1)
                        dve.wait_ge(soft_step, e + 1)
                        dve.tensor_reduce(neg_max[:], prob[:], AX.X, ALU.max, negate=True).then_inc(soft_step, 1)
                        dve.wait_ge(soft_step, e + 2)
                        dve.tensor_tensor(shift[:], neg_max[:], neg_sink[:, heads], ALU.min).then_inc(soft_step, 1)
                        dve.wait_ge(soft_step, e + 3)
                        dve.tensor_tensor(sink_in[:], shift[:], sink[:, heads], ALU.add).then_inc(shifted, 1)
                        if st == 1:
                            dve.tensor_copy(s.dist[:, 2, P:2 * P], s.dist[:, 0, P:2 * P]).then_inc(soft_step, 1)
                        else:
                            dve.sem_inc(soft_step, 1)
                    if n % 3 == 1 and n < 24:
                        st = n // 3
                        e = 6 * (STEPS * i + st)
                        dve.wait_ge(exped, 5 * (STEPS * i + st) + 5)
                        dve.wait_ge(normed, STEPS * i + st)
                        dve.tensor_tensor(denom[:], total[:], sink_e[:], ALU.add).then_inc(soft_step, 1)
                        dve.wait_ge(soft_step, e + 5)
                        dve.reciprocal(inv[:], denom[:]).then_inc(soft_step, 1)
                        if st % 2 == 1 and st < STEPS - 1:
                            q_lo_block(QB * i + st // 2 + 1)
                    if n == SLOTS - 1:
                        o_add(i, STEPS - 1)

        @block.tensor
        def _(pe):
            def turn(i, x, xt):
                cols = GROUPS[xt][1]
                pe.wait_ge(group_out, NG * (5 * i + x) + xt + 1 + AHEAD)
                if x == K and xt == 0:
                    pe.wait_ge(v_rows, NG * i)
                elif x == K or xt == 0:
                    pe.wait_ge(k_rows, NG * i + (xt if x == K else NG))
                else:
                    pe.wait_ge(v_rows, NG * i + xt)
                    pe.wait_ge(v_hi, 4 * i + min(xt, NSB))
                if x == V and xt == 0 or x == K and xt == 0:
                    pe.wait_ge(v_hi, 4 * i)
                for j in range(max(1, cols // P)):
                    r = min(cols, P)
                    src = raw[:, xt % 2, j * P:j * P + r] if xt < NSB else raw_s[:]
                    last = pe.transpose(turned_ps[0:r, j * P:(j + 1) * P], src, s.ident[:])
                last.then_inc(turned, 1)

            def take_scores(i, st):
                j, g = divmod(st, KV)
                b = QB * i + j
                pe.wait_ge(q_ready, b + 1)
                pe.wait_ge(k_ready, b + 1)
                pe.wait_ge(shifted, STEPS * i + st)
                for h in range(GROUP):
                    qh = qpart[:, GROUP * g + h, :]
                    pe.matmul(score[:, h, :], qh, khi[:, g].rearrange("p b k -> p (b k)"), start=True, stop=False)
                    last = pe.matmul(score[:, h, :], qh, klo[:, g].rearrange("p b k -> p (b k)"),
                                     start=False, stop=True)
                last.then_inc(scored, 1)

            def turn_probs(i, st, slot):
                pe.wait_ge(normed, STEPS * i + st + 1)
                pe.wait_ge(pt_lo_ready, 2 * (STEPS * i + st) + slot)
                for h in range(GROUP):
                    last = pe.transpose(pt_ps[:, h * P:(h + 1) * P], prob[:, h, slot * P:(slot + 1) * P], s.ident[:])
                last.then_inc(probs_turned, 1)

            def mix(i, st, slot):
                j, g = divmod(st, KV)
                pe.wait_ge(v_block_in, 16 * (QB * i + j + 1))
                pe.wait_ge(pt_lo_ready, 2 * (STEPS * i + st) + slot + 1)
                pe.wait_ge(o_ready, STEPS * i + st)
                pe.matmul(o_ps[:], vwin[:, slot, g, :], pt_hi[slot][:], start=(slot == 0), stop=False)
                pe.matmul(o_ps[:], vwin[:, slot, g, :], pt_lo[slot][:], start=False, stop=(slot == 1))\
                  .then_inc(mixed, 1)

            pe.wait_ge(start_done, 1)
            with pe.Fori(0, PAIRS) as i:
                for n in range(SLOTS):
                    u, t = divmod(n, NG)
                    t0, cols = GROUPS[t]
                    c = 5 * i + u
                    if t == 0:
                        pe.wait_ge(w.lo_ready, c + 1)
                    wait_bank(pe, group_out, NG * c, t)
                    if (u == K and t in (2, 3)) or (u == V and t in (0, 1)):
                        pe.wait_ge(k_lo_done, 4 * i + {(K, 2): 1, (K, 3): 2, (V, 0): 3, (V, 1): 4}[u, t])
                    project(pe, s, w, SETS[u], bank[BANK[t]][:, 0:cols], t0, cols).then_inc(group_ready, 1)
                    if turned_slot(n):
                        turn(i, *turned_slot(n))
                    if n % 3 == 2:
                        turn_probs(i, n // 3, 0)
                    if n % 3 == 0 and n:
                        mix(i, n // 3 - 1, 0)
                        turn_probs(i, n // 3 - 1, 1)
                    if n % 3 == 1 and n > 3:
                        mix(i, n // 3 - 1, 1)
                    if n == SLOTS - 1:
                        mix(i, STEPS - 1, 1)
                    if n % 3 == 0 and n < 24:
                        take_scores(i, n // 3)


class OutProjection:

    def __init__(self, nc, s, ctx):
        sb = lambda name, shape, dt=F32: ctx.enter_context(nc.sbuf_tensor(name, shape, dt))
        sem = lambda name: ctx.enter_context(nc.semaphore(name))
        self.s = s
        self.w_hi, self.w_lo = sb("wo_hi", [P, DT, D], F32R), sb("wo_lo", [P, DT, D], F32R)
        self.o, self.gate, self.x = sb("p_o", [P, DT, P]), sb("p_gate", [P, DT, P]), sb("p_x", [P, D])
        self.mixed = sb("p_mixed", [P, DT, P])
        self.m_hi, self.m_lo = sb("p_m_hi", [P, DT, P], F32R), sb("p_m_lo", [P, DT, P], F32R)
        self.y = sb("p_y", [P, D])
        self.ps = ctx.enter_context(nc.psum_tensor("p_ps", [P, D // 2], F32))
        self.w_in = [sem("wo_in0"), sem("wo_in1")]
        self.w_hi_ready, self.w_lo_ready = sem("wo_hi_ready"), sem("wo_lo_ready")
        self.loaded, self.x_loaded = sem("p_loaded"), sem("p_x_loaded")
        self.sig, self.silu, self.mix_ready = sem("p_sig"), sem("p_silu"), sem("p_mix_ready")
        self.hi_ready, self.lo_ready = sem("p_hi_ready"), sem("p_lo_ready")
        self.summed, self.y_ready, self.y_stored = sem("p_summed"), sem("p_y_ready"), sem("p_y_stored")

    def raw_w(self, e):
        return self.gate[:].rearrange("p a c -> p (a c)") if e == 0 else self.x[:]

    def load_w(self, sp, n, e):
        sp.wait_ge(self.w_lo_ready, n - e)
        sp.dma_start(self.raw_w(e), self.s.w_out[:, n, :]).then_inc(self.w_in[e], 16)

    def split_w_hi(self, act, n, e, half):
        act.wait_ge(self.w_in[e], 16 * half + 16)
        act.activation(self.w_hi[:, n, :], self.raw_w(e), ACT.Copy).then_inc(self.w_hi_ready, 1)

    def split_w_lo(self, pool, n, e):
        pool.wait_ge(self.w_hi_ready, n + 1)
        pool.tensor_tensor(self.w_lo[:, n, :], self.raw_w(e), f32(self.w_hi[:, n, :]),
                           ALU.subtract).then_inc(self.w_lo_ready, 1)

    def load(self, sp, r, cols=P):
        t0 = P * r
        sp.wait_ge(self.y_ready, 2 * r)
        sp.wait_ge(self.mix_ready, r)
        sp.wait_ge(self.w_lo_ready, DT)
        sp.dma_start(self.o[:, :, 0:cols], self.s.oT_all[:, :, bass.ds(t0, cols)]).then_inc(self.loaded, 16)
        sp.dma_start(self.gate[:, :, 0:cols], self.s.gateT_all[:, :, bass.ds(t0, cols)]).then_inc(self.loaded, 16)
        src = self.s.x_prompt[bass.ds(t0, cols), :] if cols == P else self.s.x_sample
        sp.dma_start(self.x[0:cols, :], src).then_inc(self.x_loaded, 16)

    def store(self, sp, r, cols=P):
        sp.wait_ge(self.y_ready, 2 * r + 2)
        dst = self.s.y_prompt[bass.ds(P * r, cols), :] if cols == P else self.s.y_sample
        sp.dma_start(dst, self.y[0:cols, :]).then_inc(self.y_stored, 16)

    def sigmoid(self, act, r, cols=P):
        act.wait_ge(self.loaded, 32 * r + 32)
        act.wait_ge(self.lo_ready, r)
        act.activation(self.mixed[:, :, 0:cols], self.gate[:, :, 0:cols], ACT.Sigmoid).then_inc(self.sig, 1)

    def gate_o(self, pool, r, cols=P):
        pool.wait_ge(self.sig, r + 1)
        pool.tensor_tensor(self.mixed[:, :, 0:cols], self.mixed[:, :, 0:cols], self.gate[:, :, 0:cols],
                           ALU.mult).then_inc(self.silu, 1)
        pool.wait_ge(self.silu, r + 1)
        pool.tensor_tensor(self.mixed[:, :, 0:cols], self.mixed[:, :, 0:cols], self.o[:, :, 0:cols],
                           ALU.mult).then_inc(self.mix_ready, 1)

    def split_hi(self, act, r, cols=P):
        act.wait_ge(self.mix_ready, r + 1)
        act.wait_ge(self.summed, 2 * r)
        act.activation(self.m_hi[:, :, 0:cols], self.mixed[:, :, 0:cols], ACT.Copy).then_inc(self.hi_ready, 1)

    def split_lo(self, dve, r, cols=P):
        dve.wait_ge(self.hi_ready, r + 1)
        dve.tensor_tensor(self.m_lo[:, :, 0:cols], self.mixed[:, :, 0:cols], f32(self.m_hi[:, :, 0:cols]),
                          ALU.subtract).then_inc(self.lo_ready, 1)

    def products(self, pe, r, half, tiles):
        cols = slice(half * D // 2, (half + 1) * D // 2)
        if tiles[0] == 0:
            pe.wait_ge(self.lo_ready, r + 1)
            pe.wait_ge(self.y_ready, 2 * r + half)
        for dt in tiles:
            pe.matmul(self.ps[:], self.m_hi[:, dt, :], self.w_hi[:, dt, cols], start=(dt == 0), stop=False)
            pe.matmul(self.ps[:], self.m_hi[:, dt, :], self.w_lo[:, dt, cols], start=False, stop=False)
            last = pe.matmul(self.ps[:], self.m_lo[:, dt, :], self.w_hi[:, dt, cols], start=False,
                             stop=(dt == DT - 1))
        if tiles[-1] == DT - 1:
            last.then_inc(self.summed, 1)

    def residual(self, dve, r, half, cols=P):
        c = slice(half * D // 2, (half + 1) * D // 2)
        dve.wait_ge(self.summed, 2 * r + half + 1)
        dve.wait_ge(self.x_loaded, 16 * r + 16)
        dve.wait_ge(self.y_stored, 16 * r)
        dve.tensor_tensor(self.y[0:cols, c], self.ps[0:cols, :], self.x[0:cols, c], ALU.add).then_inc(self.y_ready, 1)


def stick_breaking_stage(nc, s, proj):
    with ExitStack() as ctx:
        sb = lambda name, shape, dt=F32: ctx.enter_context(nc.sbuf_tensor(name, shape, dt))
        sem = lambda name: ctx.enter_context(nc.semaphore(name))
        qraw = [sb(f"c_qraw{e}", [P, SB]) for e in range(2)]
        q_hi = [sb(f"c_q_hi{e}", [P, SB], F32R) for e in range(2)]
        q_lo = [sb(f"c_q_lo{e}", [P, SB], F32R) for e in range(2)]
        k = [sb(f"c_k{e}", [P, NSB, SB], F32R) for e in range(2)]
        v = [sb(f"c_v{e}", [P, NSB, QB, P], F32R) for e in range(2)]
        keep = sb("c_keep", [P, 2, 2, SB])
        take = sb("c_take", [P, 2, QB, SB])
        kept = sb("c_kept", [P, 2, QB, SB + 4])
        w_hi = [sb(f"c_w_hi{n}", [P, SB], F32R) for n in range(2)]
        w_lo = [sb(f"c_w_lo{n}", [P, SB], F32R) for n in range(2)]
        o_sum = [sb(f"c_o_sum{n}", [P, SB]) for n in range(2)]
        score = [ctx.enter_context(nc.psum_tensor(f"c_score{h}", [P, 2, SB], F32)) for h in range(2)]
        turn_ps = [ctx.enter_context(nc.psum_tensor(f"c_turn{h}", [P, SB], F32)) for h in range(2)]
        o_ps = ctx.enter_context(nc.psum_tensor("c_o", [P, SB], F32))
        q_in, kv_in, more_in = ([sem(f"c_{n}{e}") for e in range(2)] for n in ("q_in", "kv_in", "more_in"))
        q_hi_ready, q_lo_ready, start_done = sem("c_q_hi_ready"), sem("c_q_lo_ready"), sem("c_start_done")
        scored, take_ready, keep_ready, scanned, carried, weighted = (
            sem("c_" + n) for n in ("scored", "take_ready", "keep_ready", "scanned", "carried", "weighted"))
        turned, hi_ready, lo_ready, mixed = (sem("c_" + n) for n in ("turned", "hi_ready", "lo_ready", "mixed"))
        o_lo_out, o_ready, o_stored = sem("c_o_lo_out"), sem("c_o_ready"), [sem("c_o_stored0"), sem("c_o_stored1")]
        block = ctx.enter_context(nc.Block())

        units = lambda q, p: 4 * q * (q + 1) + 2 * (q + 1) * p
        heads = lambda q, p: HEADS * q + 2 * p
        kv_count = lambda q, p: 2 + 4 * q * (q + 1) + 2 * (q + 1) * p

        class Step:
            def __init__(self, q, p, u):
                self.q, self.p, self.u = q, p, u
                per = q + 1
                self.ahead = u // (2 * per)
                self.e = (u // per) % 2
                self.slot = u % per if not self.ahead else 0
                self.diagonal = self.slot == 0
                self.last = not self.ahead and self.slot == q
                self.number = units(q, p) + u
                self.head = heads(q, p) + (2 if self.ahead else self.e)
                self.head_e = 4 * q + p + self.ahead
                self.kv = kv_count(q, p) + (2 * per if self.ahead else 0)
                self.par = u % 2

        def widths(st, h):
            return [(j, (P * (j + 1) if st.diagonal else SB)) for j in (2 * h, 2 * h + 1)]

        PIECES = {1: {2: [(0, 0), (0, 1)], 3: [(1, 0), (1, 1)]},
                  2: {2: [(0, 0)], 3: [(0, 1)], 4: [(1, 0)], 5: [(1, 1)]},
                  3: {3: [(0, 0)], 4: [(0, 1)], 5: [(1, 0)], 6: [(1, 1)]}, 0: {}}

        def iterations(eng, body):
            for q in range(NSB):
                if q < NSB - 1:
                    with eng.Fori(0, PAIRS) as p:
                        body(q, p, False)
                else:
                    with eng.Fori(0, PAIRS - 1) as p:
                        body(q, p, False)
                    body(q, PAIRS - 1, True)

        @block.sync
        def _(sp):
            def load_q(q, p, e, nth):
                sp.wait_ge(q_lo_ready, nth)
                n = 4 * q + p
                for half in range(2):
                    sp.dma_start(qraw[e][half * HD:(half + 1) * HD, :],
                                 s.qT_all[bass.ds(n, 1), e * HD:(e + 1) * HD, :]
                                 .rearrange("o d t -> (o d) t")).then_inc(q_in[e], 16)

            def load_kv(q, p, e, slots, sems):
                for slot in slots:
                    n = HEADS * (q - slot) + 2 * p + e
                    sp.dma_start(f32(k[e][:, slot, :]), s.k_parts_all[bass.ds(n, 1), :, :]
                                 .rearrange("o p c -> (o p) c")).then_inc(sems[e], 16)
                    sp.dma_start(f32(v[e][:, slot]).rearrange("p j c -> p (j c)"),
                                 s.v_parts_all[bass.ds(n, 1), :, :].rearrange("o p c -> (o p) c")).then_inc(sems[e], 16)

            def body(q, p, last):
                if q:
                    r = 4 * (q - 1) + p
                    for e in range(2):
                        sp.wait_ge(o_stored[e], 16 * PAIRS * q)
                    proj.load(sp, r)
                else:
                    for e in range(2):
                        proj.load_w(sp, 2 * p + e, e)
                for e in range(2):
                    head = heads(q, p) + e
                    if not last:
                        load_q(q, p + 1, e, head + 1)
                    sp.wait_ge(mixed, 4 * (units(q, p) + (e + 1) * (q + 1)))
                    if not last:
                        load_kv(q, p + 1, e, range(q + 1), kv_in)
                    sp.wait_ge(o_ready, head + 1)
                    sp.dma_start(s.oT_heads[bass.ds(2 * p + e, 1), :, SB * q:SB * (q + 1)]
                                 .rearrange("o d t -> (o d) t"), o_sum[e][0:HD, :]).then_inc(o_stored[e], 16)
                if q:
                    proj.store(sp, r)

            for e in range(2):
                load_q(0, 0, e, 0)
                load_kv(0, 0, e, [0], kv_in)
            for q in range(NSB):
                if q:
                    for e in range(2):
                        load_kv(q, 0, e, [q], more_in)
                if q < NSB - 1:
                    with sp.Fori(0, PAIRS) as p:
                        body(q, p, False)
                else:
                    with sp.Fori(0, PAIRS - 1) as p:
                        body(q, p, False)
                    body(q, PAIRS - 1, True)
            for e in range(2):
                sp.wait_ge(o_stored[e], 16 * NSB * PAIRS)
            sp.wait_ge(proj.y_stored, 16 * PAIRS * (NSB - 1))

        @block.gpsimd
        def _(pool):
            def q_lo_part(st):
                pool.wait_ge(q_hi_ready, st.head + 1)
                pool.tensor_tensor(q_lo[st.e][:], qraw[st.e][:], f32(q_hi[st.e][:]), ALU.subtract)\
                    .then_inc(q_lo_ready, 1)

            def weigh(st, h):
                pool.wait_ge(scanned, 2 * st.number + h + 1)
                pool.wait_ge(take_ready, 2 * st.number + h + 1)
                if not st.diagonal:
                    pool.wait_ge(carried, st.number + 1)
                    j = slice(2 * h, 2 * h + 2)
                    last = pool.tensor_tensor(take[:, st.par, j, :], take[:, st.par, j, :],
                                              kept[:, st.par, j, 1:SB + 1], ALU.mult)
                else:
                    for j, n in widths(st, h):
                        last = pool.tensor_tensor(take[:, st.par, j, 0:n], take[:, st.par, j, 0:n],
                                                  kept[:, st.par, j, 1:n + 1], ALU.mult)
                last.then_inc(weighted, 1)

            def body(q, p, last):
                steps = 2 * (q + 1)
                for u in range(steps):
                    nxt = Step(q, p, u + 1)
                    run = not (last and nxt.ahead)
                    for du in ((1, 2) if u == 0 else (2,)):
                        if u + du <= steps and Step(q, p, u + du).diagonal and not (last and u + du == steps):
                            q_lo_part(Step(q, p, u + du))
                    if run:
                        weigh(nxt, 0)
                    if q and u == 1:
                        proj.gate_o(pool, 4 * (q - 1) + p)
                    if not q:
                        proj.split_w_lo(pool, 2 * p + u, u)
                    if run:
                        weigh(nxt, 1)

            pool.wait_ge(start_done, 2)
            q_lo_part(Step(0, 0, 0))
            weigh(Step(0, 0, 0), 0)
            weigh(Step(0, 0, 0), 1)
            iterations(pool, body)

        @block.scalar
        def _(act):
            def q_hi_part(st, first=False):
                act.wait_ge(q_in[st.e], 32 * (st.head_e + 1))
                if not first:
                    act.wait_ge(scored, 2 * (units(st.q, st.p) + (st.q + 1 if st.ahead else 0)))
                act.activation(q_hi[st.e][:], qraw[st.e][:], ACT.Copy).then_inc(q_hi_ready, 1)

            def sigmoid_pair(st, h):
                act.wait_ge(scored, 2 * st.number + h + 1)
                out = [(j, n) for j, n in widths(st, h)]
                if st.diagonal:
                    for j, n in out:
                        last = act.activation(take[:, st.par, j, 0:n], score[h][:, j % 2, 0:n], ACT.Sigmoid,
                                              scale=SCALE)
                    last.then_inc(take_ready, 1)
                else:
                    act.activation(take[:, st.par, 2 * h:2 * h + 2, :], score[h][:], ACT.Sigmoid,
                                   scale=SCALE).then_inc(take_ready, 1)

            def front(st, h, waits=True):
                if waits:
                    act.wait_ge(turned, 4 * (st.number - 1))
                sigmoid_pair(st, h)

            def back_hi(st, n):
                act.wait_ge(turned, 4 * st.number + n + 1)
                if n > 1:
                    act.wait_ge(mixed, 4 * st.number + n - 1)
                else:
                    act.wait_ge(mixed, 4 * st.number)
                c = slice(P * n if st.diagonal else 0, SB)
                act.activation(w_hi[n % 2][:, c], turn_ps[n % 2][:, c], ACT.Copy).then_inc(hi_ready, 1)

            def finish(st):
                act.wait_ge(mixed, 4 * st.number + 4)
                act.wait_ge(o_stored[st.e], 16 * st.head_e)
                act.activation(o_sum[st.e][HD:P, :], o_ps[HD:P, :], ACT.Copy).then_inc(o_lo_out, 1)

            def body(q, p, last):
                steps = 2 * (q + 1)
                for u in range(steps):
                    st, nxt = Step(q, p, u), Step(q, p, u + 1)
                    run = not (last and nxt.ahead)
                    if q and u == 1:
                        proj.sigmoid(act, 4 * (q - 1) + p)
                    for du in ((1, 2) if u == 0 else (2,)):
                        if u + du <= steps and Step(q, p, u + du).diagonal and not (last and u + du == steps):
                            q_hi_part(Step(q, p, u + du))
                    if run:
                        front(nxt, 0)
                    back_hi(st, 0)
                    back_hi(st, 1)
                    if run:
                        front(nxt, 1)
                    back_hi(st, 2)
                    back_hi(st, 3)
                    if not q:
                        proj.split_w_hi(act, 2 * p + u, u, p)
                    if q and u == 1:
                        proj.split_hi(act, 4 * (q - 1) + p)
                    if st.last:
                        finish(st)

            act.wait_ge(start_done, 2)
            q_hi_part(Step(0, 0, 0), first=True)
            front(Step(0, 0, 0), 0, waits=False)
            front(Step(0, 0, 0), 1, waits=False)
            iterations(act, body)

        @block.vector
        def _(dve):
            def carry(st):
                dve.wait_ge(scanned, 2 * st.number)
                dve.wait_ge(weighted, 2 * st.number - 2)
                dve.tensor_copy(kept[:, st.par, :, SB:SB + 1], kept[:, 1 - st.par, :, 0:1]).then_inc(carried, 1)

            def front(st, h, waits=True):
                if waits:
                    dve.wait_ge(weighted, 2 * (st.number - 1))
                if h == 0:
                    if st.diagonal:
                        dve.sem_inc(carried, 1)
                    else:
                        carry(st)
                dve.wait_ge(take_ready, 2 * st.number + h + 1)
                n = P * (2 * h + 2) if st.diagonal else SB
                dve.tensor_scalar(keep[:, h, :, 0:n], take[:, st.par, 2 * h:2 * h + 2, 0:n], -1.0, 1.0,
                                  ALU.mult, ALU.add).then_inc(keep_ready, 1)
                dve.wait_ge(keep_ready, 2 * st.number + h + 1)
                for j, n in widths(st, h):
                    down = slice(n - 1, None, -1)
                    first = 1.0 if st.diagonal else kept[:, 1 - st.par, j, 0:1]
                    last = dve.tensor_tensor_scan(kept[:, st.par, j, down], keep[:, h, j % 2, down],
                                                  keep[:, h, j % 2, down], first, ALU.mult, ALU.bypass)
                last.then_inc(scanned, 1)

            def back_lo(st, n):
                dve.wait_ge(hi_ready, 4 * st.number + n + 1)
                c = slice(P * n if st.diagonal else 0, SB)
                dve.tensor_tensor(w_lo[n % 2][:, c], turn_ps[n % 2][:, c], f32(w_hi[n % 2][:, c]),
                                  ALU.subtract).then_inc(lo_ready, 1)

            def finish(st):
                dve.wait_ge(o_lo_out, st.head + 1)
                dve.tensor_tensor(o_sum[st.e][0:HD, :], o_ps[0:HD, :], o_sum[st.e][HD:P, :],
                                  ALU.add).then_inc(o_ready, 1)

            def body(q, p, last):
                r = 4 * (q - 1) + p
                for u in range(2 * (q + 1)):
                    st, nxt = Step(q, p, u), Step(q, p, u + 1)
                    run = not (last and nxt.ahead)
                    if run:
                        front(nxt, 0)
                    back_lo(st, 0)
                    back_lo(st, 1)
                    if run:
                        front(nxt, 1)
                    back_lo(st, 2)
                    back_lo(st, 3)
                    if q and u == 1:
                        proj.split_lo(dve, r)
                    if (0, 1) in PIECES[q].get(u, []):
                        proj.residual(dve, r, 0)
                    if (1, 1) in PIECES[q].get(u, []):
                        proj.residual(dve, r, 1)
                    if st.last:
                        finish(st)

            dve.memset(kept[:], 1.0).then_inc(start_done, 1)
            dve.memset(take[:], 0.0).then_inc(start_done, 1)
            dve.wait_ge(start_done, 2)
            front(Step(0, 0, 0), 0, waits=False)
            front(Step(0, 0, 0), 1, waits=False)
            iterations(dve, body)

        @block.tensor
        def _(pe):
            def front(st, h, waits=True):
                if waits:
                    pe.wait_ge(take_ready, 2 * (st.number - 1) + h + 1)
                if h == 0:
                    if st.diagonal:
                        pe.wait_ge(q_lo_ready, st.head + 1)
                        pe.wait_ge(kv_in[st.e], 16 * st.kv)
                    elif st.slot == st.q:
                        pe.wait_ge(more_in[st.e], 32 * st.q)
                for j, n in widths(st, h):
                    out, keys = score[h][:, j % 2, 0:n], k[st.e][:, st.slot, 0:n]
                    pe.matmul(out, q_hi[st.e][:, P * j:P * j + P], keys, start=True, stop=False)
                    last = pe.matmul(out, q_lo[st.e][:, P * j:P * j + P], keys, start=False, stop=not st.diagonal)
                    if st.diagonal:
                        last = pe.matmul(score[h][:, j % 2, n - P:n], s.ident_r[:], s.causal_r[:],
                                         start=False, stop=True)
                last.then_inc(scored, 1)

            def turn(st, n):
                if n == 0:
                    pe.wait_ge(weighted, 2 * st.number + 2)
                pe.wait_ge(lo_ready, 4 * st.number + (n - 1 if n > 1 else 0))
                for j in range(n if st.diagonal else 0, QB):
                    last = pe.transpose(turn_ps[n % 2][:, j * P:(j + 1) * P],
                                        take[:, st.par, j, n * P:(n + 1) * P], s.ident[:])
                last.then_inc(turned, 1)

            def mix(st, n):
                pe.wait_ge(lo_ready, 4 * st.number + n + 1)
                if n == 0 and st.diagonal:
                    pe.wait_ge(o_ready, st.head)
                if n == 0 and st.q and st.slot == st.q:
                    pe.wait_ge(more_in[st.e], 32 * st.q)
                c = slice(P * n if st.diagonal else 0, SB)
                end = st.last and n == QB - 1
                pe.matmul(o_ps[:, c], v[st.e][:, st.slot, n, :], w_hi[n % 2][:, c],
                          start=(st.diagonal and n == 0), stop=False)
                pe.matmul(o_ps[:, c], v[st.e][:, st.slot, n, :], w_lo[n % 2][:, c],
                          start=False, stop=end).then_inc(mixed, 1)

            def body(q, p, last):
                for u in range(2 * (q + 1)):
                    st, nxt = Step(q, p, u), Step(q, p, u + 1)
                    run = not (last and nxt.ahead)
                    if run:
                        front(nxt, 0)
                    turn(st, 0)
                    turn(st, 1)
                    if run:
                        front(nxt, 1)
                    mix(st, 0)
                    turn(st, 2)
                    mix(st, 1)
                    turn(st, 3)
                    for half, piece in PIECES[q].get(u, []):
                        proj.products(pe, 4 * (q - 1) + p, half, range(4 * piece, 4 * piece + 4))
                    mix(st, 2)
                    mix(st, 3)

            pe.wait_ge(start_done, 2)
            front(Step(0, 0, 0), 0, waits=False)
            front(Step(0, 0, 0), 1, waits=False)
            iterations(pe, body)


def sample_stage(nc, s):
    with ExitStack() as ctx:
        sb = lambda name, shape, dt=F32: ctx.enter_context(nc.sbuf_tensor(name, shape, dt))
        sem = lambda name: ctx.enter_context(nc.semaphore(name))
        PB = PAST // P
        NK = PAST + NS
        krows, vrows = sb("s_krows", [P, PB, HEADS * HD]), sb("s_vrows", [P, PB, HEADS * HD])
        vnew = sb("s_vnew", [NS, HEADS * HD])
        kT = sb("s_kT", [P, PAIRS, NK])
        qblk = sb("s_qblk", [P, PAIRS, P])
        mask = sb("s_mask", [P, NS])
        znew = sb("s_znew", [P, 2, NS])
        take, keep = sb("s_take", [P, 2, NK]), sb("s_keep", [P, 2, NK])
        kept = sb("s_kept", [P, 2, NK + 1])
        wT = sb("s_wT", [P, 2, PB + 1, P])
        oT = sb("s_oT", [P, PAIRS, NS])
        wk_rows, wv_rows, wv_new = sb("s_wk_rows", [P, P]), sb("s_wv_rows", [P, P]), sb("s_wv_new", [NS, P])
        wkT_last = sb("s_wkT_last", [P, P])
        wkT = sb("s_wkT", [P, WINDOW + NS])
        wq = sb("s_wq", [P, KV, P])
        out_rows, out_new = sb("s_out_rows", [P, P]), sb("s_out_new", [NS, P])
        dist = sb("s_dist", [NS, WINDOW + NS])
        prob = sb("s_prob", [P, KV, WINDOW + NS])
        probT, probT_new = sb("s_probT", [P, KV * P]), sb("s_probT_new", [NS, KV * P])
        sinks = sb("s_sinks", [P, HEADS])
        o_win = sb("s_o_win", [P, P])
        sink, neg_sink, neg_max, shift, sink_in, total, sink_e, denom, inv = (
            sb("s_" + n, [P, KV]) for n in ("sink", "neg_sink", "neg_max", "shift", "sink_in", "total",
                                            "sink_e", "denom", "inv"))
        turn = [ctx.enter_context(nc.psum_tensor(f"s_turn{c}", [P, SB], F32)) for c in range(PAIRS)]
        z = [ctx.enter_context(nc.psum_tensor(f"s_z{g}", [P, SB], F32)) for g in range(2)]
        z_new = ctx.enter_context(nc.psum_tensor("s_z_new", [P, SB], F32))
        win = ctx.enter_context(nc.psum_tensor("s_win", [P, SB], F32))
        cleared, k_in, v_in, q_in, w_in, direct = (
            sem("s_" + n) for n in ("cleared", "k_in", "v_in", "q_in", "w_in", "direct"))
        k_turned, kT_ready, mask_ready, scored, znew_ready, take_ready = (
            sem("s_" + n) for n in ("k_turned", "kT_ready", "mask_ready", "scored", "znew_ready", "take_ready"))
        keep_ready, scanned, weighted, w_turned, wT_ready, o_done, oT_ready = (
            sem("s_" + n) for n in ("keep_ready", "scanned", "weighted", "w_turned", "wT_ready", "o_done", "oT_ready"))
        win_turned, win_ready, win_scored, dist_ready = (
            sem("s_" + n) for n in ("win_turned", "win_ready", "win_scored", "dist_ready"))
        step, exped, prob_ready, prob_turned, probT_ready, win_done, o_win_ready = (
            sem("s_" + n) for n in ("step", "exped", "prob_ready", "prob_turned", "probT_ready", "win_done",
                                    "o_win_ready"))
        stored = sem("s_stored")
        block = ctx.enter_context(nc.Block())

        @block.sync
        def _(sp):
            sp.dma_start(krows[:], s.cache_k).then_inc(k_in, 16)
            sp.dma_start(kT[:, :, PAST:NK], s.kT_sample.rearrange("c p t -> p c t")).then_inc(q_in, 16)
            sp.wait_ge(cleared, 1)
            for e in range(2):
                for c in range(2):
                    col = (2 * c + e) * NS
                    rows = slice(e * HD, (e + 1) * HD)
                    sp.dma_start(qblk[rows, c::2, col:col + NS],
                                 s.qT_sample[c::2, rows, :].rearrange("c p t -> p c t")).then_inc(q_in, 16)
            sp.dma_start(wk_rows[:], s.cache_win_k).then_inc(w_in, 16)
            sp.dma_start(wkT_last[:], s.normT[PAIRS, :, T - WINDOW:T]).then_inc(w_in, 16)
            sp.dma_start(wkT[:, WINDOW:], s.normT[PAIRS, :, T:TT]).then_inc(w_in, 16)
            for g in range(KV):
                rows = slice(g * HD, (g + 1) * HD)
                sp.dma_start(wq[rows, g, :].rearrange("p (h t) -> p h t", h=GROUP),
                             s.normT_q[:, GROUP * g:GROUP * (g + 1), T:TT]).then_inc(w_in, 16)
            sp.dma_start(sinks[:], s.attn_sink.to_broadcast([P, HEADS])).then_inc(w_in, 16)
            sp.dma_start(vrows[:], s.cache_v).then_inc(v_in, 16)
            sp.dma_start(vnew[:], s.sb_v_sample).then_inc(v_in, 16)
            sp.dma_start(wv_rows[:], s.cache_win_v).then_inc(v_in, 16)
            sp.dma_start(wv_new[:], s.win_v_rows[T:TT, :]).then_inc(v_in, 16)
            sp.dma_start(s.win_v_prompt, s.win_v_rows[T - WINDOW:T, :]).then_inc(direct, 16)
            sp.dma_start(s.win_k_sample[0:WINDOW - NS, :], s.cache_win_k[NS:WINDOW, :]).then_inc(direct, 16)
            sp.dma_start(s.win_v_sample[0:WINDOW - NS, :], s.cache_win_v[NS:WINDOW, :]).then_inc(direct, 16)
            sp.dma_start(s.win_v_sample[WINDOW - NS:WINDOW, :], s.win_v_rows[T:TT, :]).then_inc(direct, 16)
            sp.wait_ge(win_ready, 3)
            sp.dma_start(s.win_k_prompt, out_rows[:]).then_inc(stored, 16)
            sp.dma_start(s.win_k_sample[WINDOW - NS:WINDOW, :], out_new[:]).then_inc(stored, 16)
            sp.wait_ge(oT_ready, 4)
            sp.dma_start(s.oT[0:PAIRS, :, T:TT].rearrange("c p t -> p c t"), oT[:]).then_inc(stored, 16)
            sp.wait_ge(o_win_ready, 2)
            for g in range(KV):
                sp.dma_start(s.oT_win[g, :, :, T:TT], o_win[g * HD:(g + 1) * HD, :]
                             .rearrange("p (h t) -> p h t", h=GROUP)).then_inc(stored, 16)
            sp.wait_ge(direct, 4 * 16)
            sp.wait_ge(stored, 5 * 16)

        @block.gpsimd
        def _(pool):
            for g in range(2):
                pool.wait_ge(scanned, g + 1)
                pool.tensor_tensor(take[:, g], take[:, g], kept[:, g, 1:], ALU.mult).then_inc(weighted, 1)

        @block.scalar
        def _(act):
            for c in range(0, PAIRS, 2):
                act.wait_ge(k_turned, c + 1)
                act.activation(kT[:, c, 0:PAST], turn[c][:], ACT.Copy).then_inc(kT_ready, 1)
            for g in range(2):
                act.wait_ge(scored, g + 1)
                act.activation(take[:, g, 0:PAST], z[g][:], ACT.Sigmoid, scale=SCALE).then_inc(take_ready, 1)
                act.wait_ge(znew_ready, g + 1)
                act.activation(take[:, g, PAST:], znew[:, g], ACT.Sigmoid, scale=SCALE).then_inc(take_ready, 1)
            for g in range(KV):
                act.wait_ge(step, 3 * g + 3)
                act.activation(prob[:, g], prob[:, g], ACT.Exp, bias=shift[:, g:g + 1],
                               accum_out=total[:, g:g + 1]).then_inc(exped, 1)
                act.activation(sink_e[:, g:g + 1], sink_in[:, g:g + 1], ACT.Exp).then_inc(exped, 1)
            for g in range(2):
                act.wait_ge(w_turned, g + 1)
                act.activation(wT[:, g, 0:PB, :].rearrange("p b k -> p (b k)"), turn[g][:], ACT.Copy)\
                   .then_inc(wT_ready, 1)
                act.activation(wT[0:NS, g, PB, :], turn[2 + g][0:NS, 0:P], ACT.Copy).then_inc(wT_ready, 1)

        @block.vector
        def _(dve):
            dve.memset(qblk[:], 0.0)
            dve.memset(wq[:], 0.0)
            dve.memset(kept[:], 1.0).then_inc(cleared, 1)
            for h in range(GROUP):
                last = dve.tensor_copy(mask[h * NS:(h + 1) * NS, :], s.causal[0:NS, 0:NS])
            last.then_inc(mask_ready, 1)
            dve.tensor_copy(dist[:, 0:WINDOW], s.dist[0:NS, 0, P:2 * P])
            dve.tensor_copy(dist[:, WINDOW:], s.dist[0:NS, 0, 0:NS]).then_inc(dist_ready, 1)
            for c in range(1, PAIRS, 2):
                dve.wait_ge(k_turned, c + 1)
                dve.tensor_copy(kT[:, c, 0:PAST], turn[c][:]).then_inc(kT_ready, 1)
            dve.wait_ge(win_turned, 1)
            dve.tensor_copy(wkT[:, 0:WINDOW], win[:, 0:P]).then_inc(win_ready, 1)
            dve.tensor_copy(out_rows[:], win[:, P:2 * P]).then_inc(win_ready, 1)
            dve.tensor_copy(out_new[:], win[0:NS, 2 * P:3 * P]).then_inc(win_ready, 1)
            dve.wait_ge(mask_ready, 1)
            dve.wait_ge(scored, 2)
            for g in range(2):
                dve.tensor_tensor(znew[:, g], z_new[:, g * NS:(g + 1) * NS], mask[:], ALU.add).then_inc(znew_ready, 1)
            dve.wait_ge(w_in, 6 * 16)
            for h in range(GROUP):
                rows = slice(h * NS, (h + 1) * NS)
                last = dve.tensor_copy(sink[rows, :], sinks[rows, h::GROUP])
            last.then_inc(dist_ready, 1)
            dve.wait_ge(dist_ready, 2)
            dve.tensor_scalar(neg_sink[:], sink[:], -1.0, None, ALU.mult).then_inc(dist_ready, 1)
            dve.wait_ge(dist_ready, 3)

            def scan(g):
                dve.wait_ge(take_ready, 2 * g + 2)
                dve.tensor_scalar(keep[:, g], take[:, g], -1.0, 1.0, ALU.mult, ALU.add).then_inc(keep_ready, 1)
                dve.wait_ge(keep_ready, g + 1)
                dve.tensor_tensor_scan(kept[:, g, NK - 1::-1], keep[:, g, ::-1], keep[:, g, ::-1], 1.0,
                                       ALU.mult, ALU.bypass).then_inc(scanned, 1)

            dve.wait_ge(cleared, 1)
            for g in range(KV):
                dve.wait_ge(win_scored, KV)
                for h in range(GROUP):
                    rows = slice(h * NS, (h + 1) * NS)
                    col = P + g * (WINDOW + NS)
                    last = dve.scalar_tensor_tensor(out=prob[rows, g], in0=dist[:], scalar=-SLOPE[GROUP * g + h],
                                                    in1=z_new[rows, col:col + WINDOW + NS],
                                                    op0=ALU.mult, op1=ALU.add)
                last.then_inc(prob_ready, 1)
                dve.wait_ge(prob_ready, g + 1)
                gc = slice(g, g + 1)
                dve.tensor_reduce(neg_max[:, gc], prob[:, g], AX.X, ALU.max, negate=True).then_inc(step, 1)
                dve.wait_ge(step, 3 * g + 1)
                dve.tensor_tensor(shift[:, gc], neg_max[:, gc], neg_sink[:, gc], ALU.min).then_inc(step, 1)
                dve.wait_ge(step, 3 * g + 2)
                dve.tensor_tensor(sink_in[:, gc], shift[:, gc], sink[:, gc], ALU.add).then_inc(step, 1)
                scan(g)
            dve.wait_ge(exped, 4)
            dve.tensor_tensor(denom[:], total[:], sink_e[:], ALU.add).then_inc(step, 1)
            dve.wait_ge(step, 7)
            dve.reciprocal(inv[:], denom[:]).then_inc(step, 1)
            dve.wait_ge(step, 8)
            dve.tensor_tensor(prob[:], prob[:], inv[:].unsqueeze(2).to_broadcast([P, KV, WINDOW + NS]),
                              ALU.mult).then_inc(prob_ready, 1)
            dve.wait_ge(prob_turned, 1)
            dve.tensor_copy(probT[:], win[:, 0:KV * P]).then_inc(probT_ready, 1)
            dve.tensor_copy(probT_new[:], win[0:NS, KV * P:2 * KV * P]).then_inc(probT_ready, 1)
            dve.wait_ge(o_done, PAIRS)
            for c in range(PAIRS):
                for e in range(2):
                    col = P * c + (2 * (c % 2) + e) * NS
                    last = dve.tensor_copy(oT[e * HD:(e + 1) * HD, c, :], z[0][e * HD:(e + 1) * HD, col:col + NS])
                last.then_inc(oT_ready, 1)
            dve.wait_ge(win_done, KV)
            for g in range(KV):
                rows = slice(g * HD, (g + 1) * HD)
                dve.tensor_copy(o_win[rows, :], z[1][rows, g * P:(g + 1) * P]).then_inc(o_win_ready, 1)

        @block.tensor
        def _(pe):
            pe.wait_ge(k_in, 16)
            for c in range(PAIRS):
                for b in range(PB):
                    last = pe.transpose(turn[c][:, b * P:(b + 1) * P], krows[:, b, c * P:(c + 1) * P], s.ident[:])
                last.then_inc(k_turned, 1)
            pe.wait_ge(w_in, 6 * 16)
            pe.transpose(win[:, 0:P], wk_rows[:], s.ident[:])
            pe.transpose(win[:, P:2 * P], wkT_last[:], s.ident[:])
            pe.transpose(win[0:NS, 2 * P:3 * P], wkT[:, WINDOW:], s.ident[:]).then_inc(win_turned, 1)
            pe.wait_ge(kT_ready, 4)
            pe.wait_ge(q_in, 5 * 16)
            for g in range(2):
                for c in range(2):
                    pe.matmul(z[g][:], qblk[:, 2 * g + c], kT[:, 2 * g + c, 0:PAST], start=(c == 0), stop=(c == 1))
                for c in range(2):
                    last = pe.matmul(z_new[:, g * NS:(g + 1) * NS], qblk[:, 2 * g + c], kT[:, 2 * g + c, PAST:],
                                     start=(c == 0), stop=(c == 1))
                last.then_inc(scored, 1)
            pe.wait_ge(win_ready, 3)
            pe.wait_ge(znew_ready, 2)
            for g in range(KV):
                col = P + g * (WINDOW + NS)
                pe.matmul(z_new[:, col:col + WINDOW + NS], wq[:, g], wkT[:], start=True, stop=True).then_inc(win_scored, 1)
            for g in range(2):
                pe.wait_ge(weighted, g + 1)
                for b in range(PB):
                    pe.transpose(turn[g][:, b * P:(b + 1) * P], take[:, g, b * P:(b + 1) * P], s.ident[:])
                pe.transpose(turn[2 + g][0:NS, 0:P], take[:, g, PAST:], s.ident[:]).then_inc(w_turned, 1)
            pe.wait_ge(prob_ready, 3)
            for g in range(KV):
                pe.transpose(win[:, g * P:(g + 1) * P], prob[:, g, 0:WINDOW], s.ident[:])
                last = pe.transpose(win[0:NS, (KV + g) * P:(KV + g + 1) * P], prob[:, g, WINDOW:], s.ident[:])
            last.then_inc(prob_turned, 1)
            pe.wait_ge(v_in, 4 * 16)
            pe.wait_ge(take_ready, 4)
            for c in range(PAIRS):
                g = c // 2
                pe.wait_ge(wT_ready, 2 * g + 2)
                out = z[0][:, P * c:P * (c + 1)]
                for b in range(PB):
                    pe.matmul(out, vrows[:, b, c * P:(c + 1) * P], wT[:, g, b, :], start=(b == 0), stop=False)
                pe.matmul(out, vnew[:, c * P:(c + 1) * P], wT[0:NS, g, PB, :], start=False, stop=True).then_inc(o_done, 1)
            pe.wait_ge(probT_ready, 2)
            for g in range(KV):
                cols = slice(g * P, (g + 1) * P)
                pe.matmul(z[1][:, cols], wv_rows[:], probT[:, cols], start=True, stop=False)
                pe.matmul(z[1][:, cols], wv_new[:], probT_new[:, cols], start=False, stop=True).then_inc(win_done, 1)


def tail_stage(nc, s, proj):
    with ExitStack() as ctx:
        block = ctx.enter_context(nc.Block())
        first = PAIRS * (NSB - 1)

        def blocks(eng, body):
            with eng.Fori(first, T // P) as r:
                body(r, P)
            body(T // P, NS)

        @block.sync
        def _(sp):
            def body(r, cols):
                proj.load(sp, r, cols)
                proj.store(sp, r, cols)
            blocks(sp, body)
            sp.wait_ge(proj.y_stored, 16 * (T // P + 1))

        @block.gpsimd
        def _(pool):
            blocks(pool, lambda r, cols: proj.gate_o(pool, r, cols))

        @block.scalar
        def _(act):
            def body(r, cols):
                proj.sigmoid(act, r, cols)
                proj.split_hi(act, r, cols)
            blocks(act, body)

        @block.vector
        def _(dve):
            def body(r, cols):
                proj.split_lo(dve, r, cols)
                proj.residual(dve, r, 0, cols)
                proj.residual(dve, r, 1, cols)
            blocks(dve, body)

        @block.tensor
        def _(pe):
            def body(r, cols):
                proj.products(pe, r, 0, range(DT))
                proj.products(pe, r, 1, range(DT))
            blocks(pe, body)


INPUTS = ["x_prompt", "x_sample", "cache_sb_k", "cache_sb_v", "cache_win_k", "cache_win_v",
          "norm_g", "w_in", "q_norm_g", "k_norm_g", "attn_sink", "w_out"]
OUTPUTS = [("y_prompt", (1, T, D)), ("y_sample", (1, NS, D)),
           ("sb_k_prompt", (1, 1, T, HEADS, HD)), ("sb_v_prompt", (1, 1, T, HEADS, HD)),
           ("win_k_prompt", (1, 1, WINDOW, KV, HD)), ("win_v_prompt", (1, 1, WINDOW, KV, HD)),
           ("sb_k_sample", (1, 1, NS, HEADS, HD)), ("sb_v_sample", (1, 1, NS, HEADS, HD)),
           ("win_k_sample", (1, 1, WINDOW, KV, HD)), ("win_v_sample", (1, 1, WINDOW, KV, HD))]


def build(nc, args, stages=99):
    s = Shared()
    s.x_prompt = args["x_prompt"].rearrange("b t d -> (b t) d")
    s.x_sample = args["x_sample"].rearrange("b t d -> (b t) d")
    s.norm_g, s.q_norm_g, s.k_norm_g, s.attn_sink = (args[n] for n in ("norm_g", "q_norm_g", "k_norm_g", "attn_sink"))
    s.w_in = args["w_in"].rearrange("o (a p) n -> (o p) a n", p=P)
    dram = lambda name, shape, dt=F32: nc.dram_tensor(name, shape, dt, kind="Internal").ap()
    s.normT = dram("normT", [5, P, TT])
    s.win_v_rows = dram("win_v_rows", [TT, P])
    s.win_v_parts = dram("win_v_parts", [NSB, P, QB * KV * P])
    s.normT_q = s.normT[0:PAIRS].rearrange("c (e d) t -> d (c e) t", d=HD)
    s.normT_k = s.normT[PAIRS].rearrange("(g d) t -> d g t", d=HD)
    s.qT = dram("qT", [NSB, PAIRS, P, SB])
    s.qT_sample = dram("qT_sample", [PAIRS, P, NS])
    s.kT_sample = dram("kT_sample", [PAIRS, P, NS])
    s.gateT = dram("gateT", [DT, P, TT])
    s.oT = dram("oT", [DT, P, TT])
    s.oT_win = s.oT[PAIRS:DT].rearrange("(g c) (e d) t -> g d (c e) t", g=KV, d=HD)
    s.k_parts = dram("k_parts", [NSB, HEADS, P, SB])
    s.v_parts = dram("v_parts", [NSB, HEADS, P, SB])
    s.sb_k_rows, s.sb_v_rows = (args[n].rearrange("o b (s j p) h d -> s p (o b j) (h d)", p=P, j=QB)
                                for n in ("sb_k_prompt", "sb_v_prompt"))
    s.sb_k_sample, s.sb_v_sample = (args[n].rearrange("o b t h d -> (o b t) (h d)") for n in ("sb_k_sample", "sb_v_sample"))
    s.w_out = args["w_out"].rearrange("o (a p) n -> (o p) a n", p=P)
    s.oT_all, s.gateT_all = s.oT.rearrange("a p t -> p a t"), s.gateT.rearrange("a p t -> p a t")
    s.y_prompt, s.y_sample = (args[n].rearrange("b t d -> (b t) d") for n in ("y_prompt", "y_sample"))
    s.qT_all = s.qT.rearrange("s c p t -> (s c) p t")
    s.k_parts_all, s.v_parts_all = (a.rearrange("s h p c -> (s h) p c") for a in (s.k_parts, s.v_parts))
    s.oT_heads = s.oT[0:PAIRS].rearrange("c (e d) t -> (c e) d t", d=HD)
    s.cache_k, s.cache_v = (args[n].rearrange("o b (j p) h d -> p (o b j) (h d)", p=P)
                            for n in ("cache_sb_k", "cache_sb_v"))
    s.cache_win_k, s.cache_win_v, s.win_k_prompt, s.win_v_prompt, s.win_k_sample, s.win_v_sample = (
        args[n].rearrange("o b t h d -> (o b t) (h d)") for n in (
            "cache_win_k", "cache_win_v", "win_k_prompt", "win_v_prompt", "win_k_sample", "win_v_sample"))
    with ExitStack() as ctx:
        keep = lambda name, shape, dt=F32: ctx.enter_context(nc.sbuf_tensor(name, shape, dt))
        s.ident = keep("ident", [P, P])
        s.ident_r = keep("ident_r", [P, P], F32R)
        s.causal = keep("causal", [P, P])
        s.causal_r = keep("causal_r", [P, P], F32R)
        s.ones_head = keep("ones_head", [P, P])
        s.eps = keep("eps", [P, 1])
        s.qk_gain = keep("qk_gain", [P, 2])
        s.dist = keep("dist", [P, 3, 2 * P])
        s.dist_ready = ctx.enter_context(nc.semaphore("dist_ready"))
        with ExitStack() as ctx_x:
            s.XH = ctx_x.enter_context(nc.sbuf_tensor("XH", [P, DT, TT], F32R))
            s.XL = ctx_x.enter_context(nc.sbuf_tensor("XL", [P, DT, TT], F32R))
            norm_stage(nc, s, ctx_x)
            if stages > 1:
                window_project_stage(nc, s)
            if stages > 2:
                pair_project_stage(nc, s)
        if stages > 4:
            sample_stage(nc, s)
        with ExitStack() as ctx_c:
            proj = OutProjection(nc, s, ctx_c)
            if stages > 3:
                stick_breaking_stage(nc, s, proj)
            if stages > 4:
                tail_stage(nc, s, proj)


def kernel(x_prompt, x_sample, cache_sb_k, cache_sb_v, cache_win_k, cache_win_v, norm_g, w_in,
           q_norm_g, k_norm_g, attn_sink, w_out):
    import numpy as np
    from concourse import bacc
    from concourse.bass_utils import run_bass_kernel_spmd

    arrays = dict(zip(INPUTS, map(np.asarray, (x_prompt, x_sample, cache_sb_k, cache_sb_v, cache_win_k, cache_win_v,
                                               norm_g, w_in, q_norm_g, k_norm_g, attn_sink, w_out))))
    nc = bacc.Bacc("TRN2", target_bir_lowering=False, num_devices=1)
    args = {n: nc.dram_tensor(f"in_{n}", a.shape, F32, kind="ExternalInput").ap() for n, a in arrays.items()}
    args.update({n: nc.dram_tensor(f"out_{n}", shape, F32, kind="ExternalOutput").ap() for n, shape in OUTPUTS})
    build(nc, args)
    result = run_bass_kernel_spmd(nc, [{f"in_{n}": a for n, a in arrays.items()}], core_ids=[0])
    return tuple(np.asarray(result.results[0][f"out_{n}"]) for n, _ in OUTPUTS)
```

```python
from contextlib import ExitStack

import concourse.bass as bass
from concourse import mybir

F32 = mybir.dt.float32
F32R = mybir.dt.float32r
ACT = mybir.ActivationFunctionType
ALU = mybir.AluOpType
AX = mybir.AxisListType

P = 128
T, NS, D = 2048, 32, 1024
TT = T + NS
DT = D // P
HD, HEADS, KV = 64, 8, 2
PAIRS = HEADS // 2
GROUP = HEADS // KV
SB = 512
NSB = T // SB
QB = SB // P
PAST, WINDOW = 512, 128
EPS = 1e-6
MASKED = 1e30
SCALE = HD ** -0.5
SLOPE = [2.0 ** (-8.0 * (h + 1) / HEADS) for h in range(HEADS)]
COL_Q, COL_K, COL_V, COL_G, COL_WQ, COL_WK, COL_WV, COL_WG = 0, 512, 1024, 1536, 2048, 2560, 2688, 2816


def f32(ap):
    return ap.bitcast(F32)


class Shared:
    pass


def norm_stage(nc, s, ctx_x):
    with ExitStack() as ctx:
        sb = lambda name, shape, dt=F32: ctx.enter_context(nc.sbuf_tensor(name, shape, dt))
        sem = lambda name: ctx.enter_context(nc.semaphore(name))
        x = sb("x_rows", [P, 2, QB, D])
        xs_rows = sb("xs_rows", [NS, D])
        squares = sb("squares", [P, D])
        ssq = sb("ssq", [P, 2, QB])
        rstd = sb("rstd", [P, 2, QB])
        ssq_s = sb("ssq_s", [NS, 1])
        rstd_s = sb("rstd_s", [NS, 1])
        minus_half, eps_row = sb("minus_half", [P, QB]), sb("eps_row", [P, QB])
        grow = sb("grow", [DT, P])
        qkrow = sb("qkrow", [2, P])
        gcol = sb("gcol", [P, DT])
        xs_t = sb("xs_t", [P, DT, NS])
        ps = [ctx.enter_context(nc.psum_tensor(f"xt{i}", [P, SB], F32)) for i in range(DT)]
        x_in = [sem("x_in0"), sem("x_in1")]
        small_in, consts, squared, rstd_ready = sem("small_in"), sem("consts"), sem("squared"), sem("rstd_ready")
        scaled, transposed, hi_done, lo_done = sem("scaled"), sem("transposed"), sem("hi_done"), sem("lo_done")
        g_turned, g_ready, dist_abs = sem("g_turned"), sem("g_ready"), sem("dist_abs")
        rstd_step = sem("rstd_step")
        block = ctx.enter_context(nc.Block())
        x_sb = s.x_prompt.rearrange("(s j p) d -> s p j d", p=P, j=QB)

        @block.sync
        def _(sp):
            sp.dma_start(grow[:], s.norm_g.rearrange("o (a p) -> (o a) p", p=P)).then_inc(small_in, 16)
            for half in range(2):
                sp.dma_start(qkrow[0:1, half * HD:(half + 1) * HD], s.q_norm_g).then_inc(small_in, 16)
                sp.dma_start(qkrow[1:2, half * HD:(half + 1) * HD], s.k_norm_g).then_inc(small_in, 16)
            sp.dma_start(xs_rows[:], s.x_sample).then_inc(small_in, 16)
            with sp.Fori(0, NSB // 2) as i:
                for u in range(2):
                    sp.wait_ge(transposed, 2 * DT * i)
                    sp.dma_start(x[:, u], x_sb[2 * i + u]).then_inc(x_in[u], 16)

        @block.gpsimd
        def _(pool):
            pool.memset(s.ident[:], 0.0).then_inc(consts, 1)
            pool.memset(minus_half[:], -0.5).then_inc(consts, 1)
            pool.memset(eps_row[:], EPS)
            pool.memset(s.eps[:], EPS).then_inc(consts, 1)
            pool.memset(s.causal[:], 0.0).then_inc(consts, 1)
            pool.iota(s.dist[:, 0, 0:P], [[-1, P]], base=0, channel_multiplier=1,
                      allow_small_or_imprecise_dtypes=True).then_inc(consts, 1)
            pool.iota(s.dist[:, 0, P:2 * P], [[-1, P]], base=P, channel_multiplier=1,
                      allow_small_or_imprecise_dtypes=True).then_inc(consts, 1)
            pool.wait_ge(consts, 6)
            pool.affine_select(out=s.ident[:], in_=s.ident[:], compare_op=ALU.not_equal, fill=1.0, base=0,
                               pattern=[[-1, P]], channel_multiplier=1).then_inc(consts, 1)
            pool.affine_select(out=s.causal[:], in_=s.causal[:], compare_op=ALU.is_gt, fill=-MASKED, base=0,
                               pattern=[[-1, P]], channel_multiplier=1).then_inc(consts, 1)
            pool.wait_ge(squared, 1)
            pool.tensor_tensor(rstd_s[:], ssq_s[:], eps_row[0:NS, 0:1], ALU.add).then_inc(rstd_step, 1)
            pool.wait_ge(rstd_step, 1)
            pool.tensor_tensor(rstd_s[:], rstd_s[:], minus_half[0:NS, 0:1], ALU.pow).then_inc(rstd_ready, 1)
            with pool.Fori(0, NSB // 2) as i:
                for u in range(2):
                    pool.wait_ge(squared, 2 * QB * i + QB * (u + 1) + 1)
                    pool.wait_ge(scaled, 2 * QB * i)
                    pool.tensor_tensor(rstd[:, u], ssq[:, u], eps_row[:], ALU.add).then_inc(rstd_step, 1)
                    pool.wait_ge(rstd_step, 2 * i + u + 2)
                    pool.tensor_tensor(rstd[:, u], rstd[:, u], minus_half[:], ALU.pow).then_inc(rstd_ready, 1)

        @block.scalar
        def _(act):
            act.wait_ge(small_in, 6 * 16)
            act.activation(squares[0:NS, :], xs_rows[:], ACT.Square, scale=D ** -0.5, accum_out=ssq_s[:]).then_inc(squared, 1)
            act.wait_ge(consts, 6)
            act.activation(s.dist[:, 0, :], s.dist[:, 0, :], ACT.Abs).then_inc(dist_abs, 1)
            act.wait_ge(consts, 8)
            act.activation(s.causal_r[:], s.causal[:], ACT.Copy).then_inc(dist_abs, 1)
            act.activation(s.ident_r[:], s.ident[:], ACT.Copy).then_inc(dist_abs, 1)
            act.wait_ge(g_turned, 1)
            act.activation(gcol[:], ps[0][:, 0:DT], ACT.Copy).then_inc(g_ready, 1)
            act.wait_ge(g_turned, 2)
            act.activation(s.qk_gain[:, 0:1], ps[1][:, 0:1], ACT.Copy, scale=SCALE).then_inc(g_ready, 1)
            act.activation(s.qk_gain[:, 1:2], ps[1][:, 1:2], ACT.Copy).then_inc(g_ready, 1)
            act.wait_ge(g_ready, 3)
            with act.Fori(0, NSB // 2) as i:
                for u in range(2):
                    act.wait_ge(x_in[u], 16 * i + 16)
                    for j in range(QB):
                        act.wait_ge(squared, 2 * QB * i + QB * u + j + 1)
                        act.wait_ge(rstd_step, 2 * i + 1)
                        act.activation(squares[:], x[:, u, j, :], ACT.Square, scale=D ** -0.5,
                                       accum_out=ssq[:, u, j:j + 1]).then_inc(squared, 1)
                    for dt in range(DT):
                        act.wait_ge(transposed, 2 * DT * i + DT * u + dt + 1)
                        act.activation(s.XH[:, dt, bass.ds(SB * (2 * i + u), SB)], ps[dt][:], ACT.Copy,
                                       scale=gcol[:, dt:dt + 1]).then_inc(hi_done, 1)
            act.wait_ge(lo_done, NSB * DT + 1)
            act.activation(s.XH[:, :, T:TT], xs_t[:], ACT.Copy).then_inc(hi_done, 1)

        @block.vector
        def _(dve):
            dve.memset(s.ones_head[:], 0.0).then_inc(s.dist_ready, 1)
            dve.wait_ge(s.dist_ready, 1)
            for h in range(2):
                r = slice(h * HD, (h + 1) * HD)
                dve.memset(s.ones_head[r, r], 1.0).then_inc(s.dist_ready, 1)
            dve.wait_ge(dist_abs, 1)
            dve.memset(s.dist[0:HD, 0, HD:P], MASKED).then_inc(s.dist_ready, 1)
            dve.memset(s.dist[HD:P, 0, P:P + HD], MASKED).then_inc(s.dist_ready, 1)
            dve.wait_ge(s.dist_ready, 5)
            dve.tensor_copy(s.dist[:, 1, P:2 * P], s.dist[:, 0, 0:P]).then_inc(s.dist_ready, 1)
            dve.tensor_copy(s.dist[:, 1, 0:P], s.dist[:, 0, P:2 * P]).then_inc(s.dist_ready, 1)
            dve.tensor_copy(s.dist[:, 2, 0:P], s.dist[:, 0, 0:P]).then_inc(s.dist_ready, 1)
            dve.memset(s.dist[:, 2, P:2 * P], MASKED).then_inc(s.dist_ready, 1)
            dve.wait_ge(rstd_ready, 1)
            dve.tensor_scalar(xs_rows[:], xs_rows[:], rstd_s[:], None, ALU.mult).then_inc(scaled, 1)
            dve.wait_ge(g_ready, 3)
            with dve.Fori(0, NSB // 2) as i:
                for u in range(2):
                    dve.wait_ge(rstd_ready, 2 * i + u + 2)
                    for j in range(QB):
                        dve.tensor_scalar(x[:, u, j, :], x[:, u, j, :], rstd[:, u, j:j + 1], None,
                                          ALU.mult).then_inc(scaled, 1)
                    for dt in range(DT):
                        dve.wait_ge(hi_done, 2 * DT * i + DT * u + dt + 1)
                        dve.scalar_tensor_tensor(out=s.XL[:, dt, bass.ds(SB * (2 * i + u), SB)], in0=ps[dt][:],
                                                 scalar=gcol[:, dt:dt + 1],
                                                 in1=f32(s.XH[:, dt, bass.ds(SB * (2 * i + u), SB)]),
                                                 op0=ALU.mult, op1=ALU.subtract).then_inc(lo_done, 1)
            dve.wait_ge(transposed, NSB * DT + 1)
            dve.tensor_tensor(xs_t[:], ps[0][:, 0:DT * NS].rearrange("p (a t) -> p a t", a=DT),
                              gcol[:].unsqueeze(2).to_broadcast([P, DT, NS]), ALU.mult).then_inc(lo_done, 1)
            dve.wait_ge(hi_done, NSB * DT + 1)
            dve.tensor_tensor(s.XL[:, :, T:TT], xs_t[:], f32(s.XH[:, :, T:TT]), ALU.subtract).then_inc(lo_done, 1)

        @block.tensor
        def _(pe):
            pe.wait_ge(consts, 7)
            pe.wait_ge(small_in, 6 * 16)
            pe.transpose(ps[0][:, 0:DT], grow[:], s.ident[0:DT, 0:DT]).then_inc(g_turned, 1)
            pe.transpose(ps[1][:, 0:2], qkrow[:], s.ident[0:2, 0:2]).then_inc(g_turned, 1)
            pe.wait_ge(g_ready, 3)
            with pe.Fori(0, NSB // 2) as i:
                for u in range(2):
                    pe.wait_ge(scaled, 2 * QB * i + QB * (u + 1) + 1)
                    for dt in range(DT):
                        pe.wait_ge(lo_done, 2 * DT * i + (dt + 1 if u else 0))
                        for j in range(QB):
                            last = pe.transpose(ps[dt][:, j * P:(j + 1) * P], x[:, u, j, dt * P:(dt + 1) * P],
                                                s.ident[:])
                        last.then_inc(transposed, 1)
            pe.wait_ge(lo_done, NSB * DT)
            for dt in range(DT):
                last = pe.transpose(ps[0][:, dt * NS:(dt + 1) * NS], xs_rows[:, dt * P:(dt + 1) * P],
                                    s.ident[0:NS, 0:NS])
            last.then_inc(transposed, 1)


def weight_parts(nc, ctx, tag, sets):
    w = Shared()
    w.raw = ctx.enter_context(nc.sbuf_tensor(f"{tag}_w_raw", [P, DT, P], F32))
    w.hi = [ctx.enter_context(nc.sbuf_tensor(f"{tag}_w_hi{n}", [P, DT, P], F32R)) for n in range(sets)]
    w.lo = [ctx.enter_context(nc.sbuf_tensor(f"{tag}_w_lo{n}", [P, DT, P], F32R)) for n in range(sets)]
    w.raw_in, w.hi_ready, w.lo_ready = (
        ctx.enter_context(nc.semaphore(f"{tag}_w_{n}")) for n in ("raw_in", "hi_ready", "lo_ready"))
    return w


def load_weights(sp, s, w, c, col):
    sp.wait_ge(w.lo_ready, c)
    sp.dma_start(w.raw[:], s.w_in[:, :, bass.ds(col, P)]).then_inc(w.raw_in, 16)


def split_weights_hi(act, w, c, n, group_ready, groups):
    act.wait_ge(w.raw_in, 16 * c + 16)
    act.wait_ge(group_ready, groups)
    act.activation(w.hi[n][:], w.raw[:], ACT.Copy).then_inc(w.hi_ready, 1)


def split_weights_lo(pool, w, c, n):
    pool.wait_ge(w.hi_ready, c + 1)
    pool.tensor_tensor(w.lo[n][:], w.raw[:], f32(w.hi[n][:]), ALU.subtract).then_inc(w.lo_ready, 1)


def project(pe, s, w, n, out, t0, cols):
    for dt in range(DT):
        xh, xl = s.XH[:, dt, t0:t0 + cols], s.XL[:, dt, t0:t0 + cols]
        pe.matmul(out, w.hi[n][:, dt, :], xh, start=(dt == 0), stop=False)
        pe.matmul(out, w.hi[n][:, dt, :], xl, start=False, stop=False)
        last = pe.matmul(out, w.lo[n][:, dt, :], xh, start=False, stop=(dt == DT - 1))
    return last


GROUPS = [(SB * t, SB) for t in range(NSB)] + [(T, NS)]
NG = len(GROUPS)
BANK = [0, 1, 0, 1, 2]
AHEAD = 2


def wait_bank(pe, group_free, first, t):
    back = {0: 3, 1: 3, 2: 2, 3: 2, 4: NG}[t]
    pe.wait_ge(group_free, first + t - back + 1 + AHEAD)


def window_project_stage(nc, s):
    with ExitStack() as ctx:
        sb = lambda name, shape, dt=F32: ctx.enter_context(nc.sbuf_tensor(name, shape, dt))
        sem = lambda name: ctx.enter_context(nc.semaphore(name))
        w = weight_parts(nc, ctx, "a", 2)
        sq = sb("a_sq", [P, 2, SB])
        raw = sb("a_raw", [P, 2, SB])
        root = sb("a_root", [P, SB])
        inv = sb("a_inv", [P, SB])
        nst = sb("a_nst", [P, 2, SB])
        vrow = sb("a_vrow", [P, QB, P])
        vpart = sb("a_vpart", [P, QB, KV, P], F32R)
        bank = [ctx.enter_context(nc.psum_tensor(f"a_ps{i}", [P, SB], F32)) for i in range(5)]
        sums = bank[3:5]
        group_ready, group_free = sem("a_group_ready"), sem("a_group_free")
        squared, summed, rooted, inverted = sem("a_squared"), sem("a_summed"), sem("a_rooted"), sem("a_inverted")
        normed, stored = sem("a_normed"), [sem("a_stored0"), sem("a_stored1")]
        v_raw, v_turned, v_rows, v_hi, v_lo, v_stored = (
            sem("a_" + n) for n in ("v_raw", "v_turned", "v_rows", "v_hi", "v_lo", "v_stored"))
        block = ctx.enter_context(nc.Block())
        QC = 4

        @block.sync
        def _(sp):
            def chunk(c, u):
                load_weights(sp, s, w, c + 1, COL_WQ + P * (c + 1))
                for t, (t0, n) in enumerate(GROUPS):
                    g = (NG * u + t) % 2
                    sp.wait_ge(normed, NG * c + t + 1 + AHEAD)
                    sp.dma_start(s.normT[c, :, t0:t0 + n], nst[:, g, 0:n]).then_inc(stored[g], 16)

            load_weights(sp, s, w, 0, COL_WQ)
            with sp.Fori(0, QC // 2) as i:
                for u in range(2):
                    chunk(2 * i + u, u)
            chunk(QC, 0)
            for t, (t0, n) in enumerate(GROUPS):
                sp.wait_ge(v_rows, t + 1)
                if t < NSB:
                    sp.dma_start(s.win_v_rows[t0:t0 + n, :].rearrange("(j p) c -> p j c", p=P),
                                 vrow[:]).then_inc(v_stored, 16)
                    sp.wait_ge(v_lo, t + 1)
                    sp.dma_start(s.win_v_parts[t], f32(vpart[:].rearrange("p j g c -> p (j g c)"))).then_inc(v_stored, 16)
                else:
                    sp.dma_start(s.win_v_rows[t0:t0 + n, :], vrow[0:NS, 0, :]).then_inc(v_stored, 16)
            sp.wait_ge(v_stored, (2 * NSB + 1) * 16)
            sp.wait_ge(stored[0], 13 * 16)
            sp.wait_ge(stored[1], 12 * 16)

        @block.gpsimd
        def _(pool):
            with pool.Fori(0, QC // 2 + 1) as i:
                for u in range(2):
                    split_weights_lo(pool, w, 2 * i + u, u)
            for t in range(NSB):
                pool.wait_ge(v_hi, t + 1)
                pool.wait_ge(v_rows, t + 1)
                pool.tensor_tensor(vpart[:, :, :, HD:P], vrow[:].rearrange("p j (g c) -> p j g c", g=KV),
                                   f32(vpart[:, :, :, 0:HD]), ALU.subtract).then_inc(v_lo, 1)

        @block.scalar
        def _(act):
            act.sem_inc(group_free, AHEAD)
            act.sem_inc(rooted, AHEAD)

            def roots(m, n, g):
                act.wait_ge(summed, m + 1)
                act.wait_ge(inverted, m)
                act.activation(root[:, 0:n], sums[g][:, 0:n], ACT.Sqrt, scale=1.0 / HD,
                               bias=s.eps[:]).then_inc(rooted, 1)

            def chunk(c, u):
                first = NG * c
                for t, (t0, n) in enumerate(GROUPS):
                    m, g = first + t, (NG * u + t) % 2
                    act.wait_ge(group_ready, m + 1)
                    act.wait_ge(normed, m - 1 + AHEAD)
                    act.wait_ge(rooted, m - 1 + AHEAD)
                    act.activation(sq[:, g, 0:n], bank[BANK[t]][:, 0:n], ACT.Square).then_inc(squared, 1)
                    act.activation(raw[:, g, 0:n], bank[BANK[t]][:, 0:n], ACT.Copy).then_inc(group_free, 1)
                    if t == 1:
                        split_weights_hi(act, w, c + 1, (u + 1) % 2, group_ready, NG * c)
                    if t:
                        roots(m - 1, GROUPS[t - 1][1], 1 - g)
                roots(first + NG - 1, NS, (NG * u + NG - 1) % 2)

            split_weights_hi(act, w, 0, 0, group_ready, 0)
            with act.Fori(0, QC // 2) as i:
                for u in range(2):
                    chunk(2 * i + u, u)
            chunk(QC, 0)
            for t, (t0, n) in enumerate(GROUPS):
                act.wait_ge(group_ready, NG * (QC + 1) + t + 1)
                act.wait_ge(normed, NG * (QC + 1) + AHEAD)
                act.wait_ge(v_turned, t)
                act.activation(raw[:, 0, 0:n], bank[BANK[t]][:, 0:n], ACT.Copy).then_inc(v_raw, 1)
                act.wait_ge(v_turned, t + 1)
                act.wait_ge(v_stored, 32 * t)
                if t < NSB:
                    act.activation(vrow[:].rearrange("p j c -> p (j c)"), sums[0][:], ACT.Copy).then_inc(v_rows, 1)
                    act.activation(vpart[:, :, :, 0:HD], sums[0][:].rearrange("p (j g c) -> p j g c", g=KV, c=HD),
                                   ACT.Copy).then_inc(v_hi, 1)
                else:
                    act.activation(vrow[0:NS, 0, :], sums[0][0:NS, 0:P], ACT.Copy).then_inc(v_rows, 1)

        @block.vector
        def _(dve):
            dve.sem_inc(normed, AHEAD)

            def chunk(c, u, stores, gain):
                for t, (t0, n) in enumerate(GROUPS):
                    m, g = NG * c + t, (NG * u + t) % 2
                    dve.wait_ge(rooted, m + 1 + AHEAD)
                    dve.wait_ge(normed, m + AHEAD)
                    dve.reciprocal(inv[:, 0:n], root[:, 0:n]).then_inc(inverted, 1)
                    dve.wait_ge(inverted, m + 1)
                    dve.wait_ge(stored[g], 16 * (stores + (NG * u + t) // 2))
                    dve.wait_ge(group_free, m + 1 + AHEAD)
                    dve.scalar_tensor_tensor(out=nst[:, g, 0:n], in0=raw[:, g, 0:n], scalar=gain,
                                             in1=inv[:, 0:n], op0=ALU.mult, op1=ALU.mult).then_inc(normed, 1)

            with dve.Fori(0, QC // 2) as i:
                for u in range(2):
                    chunk(2 * i + u, u, NG * i, s.qk_gain[:, 0:1])
            chunk(QC, 0, NG * QC // 2, s.qk_gain[:, 1:2])

        @block.tensor
        def _(pe):
            def sum_squares(m, n, g):
                pe.wait_ge(squared, m + 1)
                pe.wait_ge(rooted, m - 1 + AHEAD)
                pe.matmul(sums[g][:, 0:n], s.ones_head[:], sq[:, g, 0:n], start=True, stop=True).then_inc(summed, 1)

            def chunk(c, u):
                first = NG * c
                pe.wait_ge(w.lo_ready, c + 1)
                for t, (t0, n) in enumerate(GROUPS):
                    wait_bank(pe, group_free, first, t)
                    project(pe, s, w, u % 2, bank[BANK[t]][:, 0:n], t0, n).then_inc(group_ready, 1)
                    if t:
                        sum_squares(first + t - 1, GROUPS[t - 1][1], (NG * u + t - 1) % 2)
                sum_squares(first + NG - 1, NS, (NG * u + NG - 1) % 2)

            with pe.Fori(0, QC // 2) as i:
                for u in range(2):
                    chunk(2 * i + u, u)
            chunk(QC, 0)
            first = NG * (QC + 1)
            pe.wait_ge(w.lo_ready, QC + 2)

            def turn_v(t, n):
                pe.wait_ge(v_raw, t + 1)
                pe.wait_ge(rooted, first + AHEAD)
                pe.wait_ge(v_rows, t)
                pe.wait_ge(v_hi, t)
                for j in range(max(1, n // P)):
                    rows = min(n, P)
                    last = pe.transpose(sums[0][0:rows, j * P:(j + 1) * P], raw[:, 0, j * P:j * P + rows], s.ident[:])
                last.then_inc(v_turned, 1)

            for t, (t0, n) in enumerate(GROUPS):
                if t < 2:
                    wait_bank(pe, group_free, first, t)
                elif t < NSB:
                    pe.wait_ge(v_raw, t - 1)
                project(pe, s, w, 1, bank[BANK[t]][:, 0:n], t0, n).then_inc(group_ready, 1)
                if t:
                    turn_v(t - 1, GROUPS[t - 1][1])
            turn_v(NG - 1, NS)


def pair_project_stage(nc, s):
    with ExitStack() as ctx:
        sb = lambda name, shape, dt=F32: ctx.enter_context(nc.sbuf_tensor(name, shape, dt))
        sem = lambda name: ctx.enter_context(nc.semaphore(name))
        K, V, Q, G, WG = range(5)
        SETS = [0, 1, 2, 0, 1]
        COLS = [COL_K, COL_V, COL_Q, COL_G, COL_WG]
        SLOTS, STEPS = 5 * NG, 2 * QB
        w = weight_parts(nc, ctx, "b", 3)
        raw = sb("b_raw", [P, 2, SB])
        raw_s = sb("b_raw_s", [P, NS])
        rows = sb("b_rows", [P, QB, P])
        kpart = sb("b_kpart", [P, 2, SB], F32R)
        vpart = sb("b_vpart", [P, 2, QB, P], F32R)
        qraw = sb("b_qraw", [P, HEADS, P])
        qpart = sb("b_qpart", [P, HEADS, P], F32R)
        kraw = sb("b_kraw", [P, KV, P])
        khi = sb("b_khi", [P, KV, 2, P], F32R)
        klo = sb("b_klo", [P, KV, 2, P], F32R)
        vwin = sb("b_vwin", [P, 2, KV, P], F32R)
        prob = sb("b_prob", [P, GROUP, 2 * P])
        pt_hi = [sb(f"b_pt_hi{n}", [P, GROUP * P], F32R) for n in range(2)]
        pt_lo = [sb(f"b_pt_lo{n}", [P, GROUP * P], F32R) for n in range(2)]
        o_sum = sb("b_o_sum", [P, GROUP * P])
        sink = sb("b_sink", [P, HEADS])
        neg_sink = sb("b_neg_sink", [P, HEADS])
        neg_max, shift, sink_in, sink_e, total, denom, inv = (
            sb("b_" + n, [P, GROUP]) for n in ("neg_max", "shift", "sink_in", "sink_e", "total", "denom", "inv"))
        bank = [ctx.enter_context(nc.psum_tensor(f"b_ps{i}", [P, SB], F32)) for i in range(3)]
        turned_ps = ctx.enter_context(nc.psum_tensor("b_turned", [P, SB], F32))
        score = ctx.enter_context(nc.psum_tensor("b_score", [P, GROUP, 2 * P], F32))
        pt_ps = ctx.enter_context(nc.psum_tensor("b_pt", [P, GROUP * P], F32))
        o_ps = ctx.enter_context(nc.psum_tensor("b_o", [P, GROUP * P], F32))
        group_ready, group_out, k_lo_done = sem("b_group_ready"), sem("b_group_out"), sem("b_k_lo_done")
        k_hi_ready = sem("b_k_hi_ready")
        turned, k_rows, v_rows, v_hi, v_lo = (sem("b_" + n) for n in ("turned", "k_rows", "v_rows", "v_hi", "v_lo"))
        raw_stored, raw_s_stored = [sem("b_raw_stored0"), sem("b_raw_stored1")], sem("b_raw_s_stored")
        rows_stored, kpart_stored, vpart_stored = sem("b_rows_stored"), sem("b_kpart_stored"), sem("b_vpart_stored")
        sinks_in, block_in, v_block_in = sem("b_sinks_in"), sem("b_block_in"), sem("b_v_block_in")
        q_hi, q_ready, k_hi, k_ready, start_done = (
            sem("b_" + n) for n in ("q_hi", "q_ready", "k_hi", "k_ready", "start_done"))
        scored, shifted, exped, normed = (
            sem("b_" + n) for n in ("scored", "shifted", "exped", "normed"))
        soft_step, sink_ready = sem("b_soft_step"), sem("b_sink_ready")
        probs_turned, pt_hi_ready, pt_lo_ready, mixed = (
            sem("b_" + n) for n in ("probs_turned", "pt_hi_ready", "pt_lo_ready", "mixed"))
        o_lo_out, o_ready, o_stored = sem("b_o_lo_out"), sem("b_o_ready"), sem("b_o_stored")
        block = ctx.enter_context(nc.Block())

        def buffer_free(eng, i, u, t):
            if t == NG - 1:
                if u == V:
                    eng.wait_ge(turned, 10 * i + NG)
                if u == Q:
                    eng.wait_ge(turned, 10 * i + 2 * NG)
                eng.wait_ge(raw_s_stored, 16 * (4 * i + {K: 0, V: 1, Q: 1, G: 2, WG: 3}[u]))
            elif 5 * u + t in (0, 1):
                eng.wait_ge(raw_stored[t], 16 * 6 * i)
            elif 5 * u + t <= 5 * Q + 1:
                back = {(K, 2): 1, (K, 3): 2, (V, 0): 3, (V, 1): 4, (V, 2): 6, (V, 3): 7, (Q, 0): 8, (Q, 1): 9}
                eng.wait_ge(turned, 10 * i + back[u, t])
            else:
                eng.wait_ge(raw_stored[t % 2], 16 * (6 * i + 2 * (u - Q) + t // 2))

        def turned_slot(n):
            return (divmod(n - 1, NG)) if 1 <= n <= 2 * NG else None

        @block.sync
        def _(sp):
            sp.dma_start(sink[:], s.attn_sink.to_broadcast([P, HEADS])).then_inc(sinks_in, 16)
            load_weights(sp, s, w, 0, COL_K)

            def load_block(b, i, j):
                sp.wait_ge(q_ready, b)
                sp.wait_ge(k_ready, b)
                for half in range(2):
                    r = slice(half * HD, (half + 1) * HD)
                    sp.dma_start(qraw[r], s.normT_q[:, :, bass.ds(P * b, P)]).then_inc(block_in, 16)
                    sp.dma_start(kraw[r], s.normT_k[:, :, bass.ds(P * b, P)]).then_inc(block_in, 16)

            def load_v_block(b, i, j):
                sp.wait_ge(mixed, 4 * b)
                sp.dma_start(f32(vwin[:, j % 2]).rearrange("p g c -> p (g c)"),
                             s.win_v_parts[i, :, j * KV * P:(j + 1) * KV * P]).then_inc(v_block_in, 16)

            with sp.Fori(0, PAIRS) as i:
                load_block(QB * i, i, 0)
                load_v_block(QB * i, i, 0)
                for n in range(SLOTS):
                    u, t = divmod(n, NG)
                    t0, cols = GROUPS[t]
                    c = 5 * i + u
                    if t == 0:
                        load_weights(sp, s, w, c + 1, COLS[(u + 1) % 5] + P * (i + (u == 4)))
                    if n % 6 == 3 and n < 21:
                        load_block(QB * i + n // 6 + 1, i, n // 6 + 1)
                    if u in (Q, G, WG):
                        sp.wait_ge(group_out, NG * c + t + 1 + AHEAD)
                        if u == Q:
                            out = s.qT[t, i] if t < NSB else s.qT_sample[i]
                        else:
                            out = s.gateT[i + (PAIRS if u == WG else 0), :, t0:t0 + cols]
                        if t < NSB:
                            sp.dma_start(out, raw[:, t % 2, :]).then_inc(raw_stored[t % 2], 16)
                        else:
                            sp.dma_start(out, raw_s[:]).then_inc(raw_s_stored, 16)
                    if u == K and t == NG - 1:
                        sp.wait_ge(group_out, NG * c + t + 1 + AHEAD)
                        sp.dma_start(s.kT_sample[i], raw_s[:]).then_inc(raw_s_stored, 16)
                    parts = sp.snap(sp.to_reg(4 * i + t + 1)) if n == 1 else 4 * i + t + 1
                    if n == 1:
                        sp.wait_ge(k_rows, NG * i + 1)
                    if u == K and t < NSB:
                        sp.wait_ge(k_lo_done, parts)
                        sp.dma_start(s.k_parts[t, bass.ds(2 * i, 2)].rearrange("h p c -> p h c"),
                                     f32(kpart[:])).then_inc(kpart_stored, 16)
                    if turned_slot(n):
                        x, xt = turned_slot(n)
                        if n > 1:
                            sp.wait_ge(v_rows if x == V else k_rows, NG * i + xt + 1)
                        big, small = (s.sb_v_rows, s.sb_v_sample) if x == V else (s.sb_k_rows, s.sb_k_sample)
                        if xt < NSB:
                            sp.dma_start(big[xt, :, :, bass.ds(P * i, P)], rows[:]).then_inc(rows_stored, 16)
                        else:
                            sp.dma_start(small[:, bass.ds(P * i, P)], rows[0:NS, 0, :]).then_inc(rows_stored, 16)
                        if x == V and xt < NSB:
                            sp.wait_ge(v_lo, 4 * i + xt + 1)
                            sp.dma_start(s.v_parts[xt, bass.ds(2 * i, 2)].rearrange("h p c -> p h c"),
                                         f32(vpart[:]).rearrange("p h j c -> p h (j c)")).then_inc(vpart_stored, 16)
                    if (n >= 4 and (n - 4) % 3 == 0) or n == SLOTS - 1:
                        st = 7 if n == SLOTS - 1 else (n - 4) // 3
                        j, g = divmod(st, KV)
                        sp.wait_ge(o_ready, STEPS * i + st + 1)
                        sp.dma_start(s.oT_win[g, :, :, bass.ds(P * (QB * i + j), P)],
                                     o_sum[0:HD].rearrange("p (h t) -> p h t", h=GROUP)).then_inc(o_stored, 16)
                        if g == 1 and j < QB - 1:
                            load_v_block(QB * i + j + 1, i, j + 1)
            for q, count in ((raw_stored[0], 6 * PAIRS), (raw_stored[1], 6 * PAIRS), (raw_s_stored, 4 * PAIRS),
                             (rows_stored, 10 * PAIRS), (kpart_stored, 4 * PAIRS), (vpart_stored, 4 * PAIRS),
                             (o_stored, STEPS * PAIRS)):
                sp.wait_ge(q, 16 * count)

        @block.gpsimd
        def _(pool):
            def k_lo_block(b, j):
                pool.wait_ge(k_hi, b + 1)
                pool.tensor_tensor(klo[:, :, j % 2, :], kraw[:], f32(khi[:, :, j % 2, :]),
                                   ALU.subtract).then_inc(k_ready, 1)

            split_weights_lo(pool, w, 0, 0)
            pool.wait_ge(start_done, 1)
            with pool.Fori(0, PAIRS) as i:
                k_lo_block(QB * i, 0)
                for n in range(SLOTS):
                    u, t = divmod(n, NG)
                    if t == 1:
                        split_weights_lo(pool, w, 5 * i + u + 1, SETS[(u + 1) % 5])
                    if turned_slot(n) and turned_slot(n)[0] == V and turned_slot(n)[1] < NSB:
                        xt = turned_slot(n)[1]
                        pool.wait_ge(v_hi, 4 * i + xt + 1)
                        pool.tensor_tensor(vpart[:, :, :, HD:P], rows[:].rearrange("p j (h c) -> p h j c", h=2),
                                           f32(vpart[:, :, :, 0:HD]), ALU.subtract).then_inc(v_lo, 1)
                    if n % 3 == 1 and n < 24:
                        st = n // 3
                        if st % 2 == 1 and st < STEPS - 1:
                            k_lo_block(QB * i + st // 2 + 1, st // 2 + 1)

        @block.scalar
        def _(act):
            def split_block(b, j):
                act.wait_ge(block_in, 64 * (b + 1))
                act.wait_ge(scored, 2 * b)
                act.activation(qpart[:], qraw[:], ACT.Copy).then_inc(q_hi, 1)
                act.activation(khi[:, :, j % 2, :], kraw[:], ACT.Copy).then_inc(k_hi, 1)

            def pt_hi_copy(i, st, slot):
                act.wait_ge(probs_turned, 2 * (STEPS * i + st) + slot + 1)
                act.wait_ge(mixed, 2 * (STEPS * i + st))
                act.activation(pt_hi[slot][:], pt_ps[:], ACT.Copy).then_inc(pt_hi_ready, 1)

            def o_copy(i, st):
                act.wait_ge(mixed, 2 * (STEPS * i + st) + 2)
                act.wait_ge(o_stored, 16 * (STEPS * i + st))
                act.activation(o_sum[HD:P, :], o_ps[HD:P, :], ACT.Copy).then_inc(o_lo_out, 1)

            act.sem_inc(group_out, AHEAD)
            split_weights_hi(act, w, 0, 0, group_ready, 0)
            act.wait_ge(start_done, 1)
            with act.Fori(0, PAIRS) as i:
                split_block(QB * i, 0)
                for n in range(SLOTS):
                    u, t = divmod(n, NG)
                    t0, cols = GROUPS[t]
                    m = NG * (5 * i + u) + t
                    ps = bank[BANK[t]]
                    act.wait_ge(group_ready, m + 1)
                    buffer_free(act, i, u, t)
                    out = raw[:, t % 2, :] if t < NSB else raw_s[:]
                    last = act.activation(out, ps[:, 0:cols], ACT.Copy)
                    if u == K and t < NSB:
                        act.wait_ge(kpart_stored, 16 * (4 * i + t))
                        act.activation(kpart[0:HD, 0, :], ps[0:HD, :], ACT.Copy).then_inc(k_hi_ready, 1)
                        last = act.activation(kpart[0:HD, 1, :], ps[HD:P, :], ACT.Copy)
                    last.then_inc(group_out, 1)
                    if t == 1:
                        split_weights_hi(act, w, 5 * i + u + 1, SETS[(u + 1) % 5], group_ready, NG * (5 * i + u))
                    if turned_slot(n) and turned_slot(n)[0] == V:
                        xt = turned_slot(n)[1]
                        act.wait_ge(turned, 10 * i + NG + xt + 1)
                        act.wait_ge(rows_stored, 16 * (10 * i + NG + xt))
                        if xt < NSB:
                            act.wait_ge(v_lo, 4 * i + xt)
                            act.activation(rows[:].rearrange("p j c -> p (j c)"), turned_ps[:], ACT.Copy)\
                               .then_inc(v_rows, 1)
                            act.wait_ge(vpart_stored, 16 * (4 * i + xt))
                            act.activation(vpart[:, :, :, 0:HD],
                                           turned_ps[:].rearrange("p (j h c) -> p h j c", h=2, c=HD),
                                           ACT.Copy).then_inc(v_hi, 1)
                        else:
                            act.wait_ge(v_lo, 4 * i + NSB)
                            act.activation(rows[0:NS, 0, :], turned_ps[0:NS, 0:P], ACT.Copy).then_inc(v_rows, 1)
                    if n % 3 == 1 and n < 24:
                        st = n // 3
                        if st:
                            o_copy(i, st - 1)
                        act.wait_ge(shifted, STEPS * i + st + 1)
                        for h in range(GROUP):
                            act.activation(prob[:, h, :], prob[:, h, :], ACT.Exp, bias=shift[:, h:h + 1],
                                           accum_out=total[:, h:h + 1]).then_inc(exped, 1)
                        act.activation(sink_e[:], sink_in[:], ACT.Exp).then_inc(exped, 1)
                        if st % 2 == 1 and st < STEPS - 1:
                            split_block(QB * i + st // 2 + 1, st // 2 + 1)
                    if n % 3 == 2:
                        pt_hi_copy(i, n // 3, 0)
                    if n % 3 == 0 and n:
                        pt_hi_copy(i, n // 3 - 1, 1)
                    if n == SLOTS - 1:
                        o_copy(i, STEPS - 1)

        @block.vector
        def _(dve):
            def q_lo_block(b):
                dve.wait_ge(q_hi, b + 1)
                dve.tensor_tensor(qpart[HD:P], qraw[HD:P], f32(qpart[HD:P]), ALU.subtract).then_inc(q_ready, 1)

            def pt_lo_copy(i, st, slot):
                dve.wait_ge(pt_hi_ready, 2 * (STEPS * i + st) + slot + 1)
                dve.tensor_tensor(pt_lo[slot][:], pt_ps[:], f32(pt_hi[slot][:]), ALU.subtract).then_inc(pt_lo_ready, 1)

            def o_add(i, st):
                dve.wait_ge(o_lo_out, STEPS * i + st + 1)
                dve.tensor_tensor(o_sum[0:HD, :], o_ps[0:HD, :], o_sum[HD:P, :], ALU.add).then_inc(o_ready, 1)

            dve.memset(f32(khi[:, :, 1, :]), 0.0)
            dve.memset(f32(klo[:, :, 1, :]), 0.0)
            dve.memset(f32(vwin[:, 1]), 0.0).then_inc(start_done, 1)
            dve.wait_ge(sinks_in, 16)
            dve.tensor_scalar(neg_sink[:], sink[:], -1.0, None, ALU.mult).then_inc(sink_ready, 1)
            dve.wait_ge(sink_ready, 1)
            with dve.Fori(0, PAIRS) as i:
                q_lo_block(QB * i)
                for n in range(SLOTS):
                    u, t = divmod(n, NG)
                    if u == K and t < NSB:
                        for h in range(2):
                            if h == 0:
                                dve.wait_ge(k_hi_ready, 4 * i + t + 1)
                            else:
                                dve.wait_ge(group_out, NG * (5 * i + u) + t + 1 + AHEAD)
                            last = dve.tensor_tensor(kpart[HD:P, h, :], bank[BANK[t]][h * HD:(h + 1) * HD, :],
                                                     f32(kpart[0:HD, h, :]), ALU.subtract)
                        last.then_inc(k_lo_done, 1)
                    if turned_slot(n) and turned_slot(n)[0] == K:
                        xt = turned_slot(n)[1]
                        dve.wait_ge(turned, 10 * i + xt + 1)
                        dve.wait_ge(rows_stored, 16 * (10 * i + xt))
                        if xt < NSB:
                            if xt == 0:
                                dve.wait_ge(v_lo, 4 * i)
                            dve.tensor_copy(rows[:].rearrange("p j c -> p (j c)"), turned_ps[:]).then_inc(k_rows, 1)
                        else:
                            dve.tensor_copy(rows[0:NS, 0, :], turned_ps[0:NS, 0:P]).then_inc(k_rows, 1)
                    if n % 3 == 2:
                        pt_lo_copy(i, n // 3, 0)
                    if n % 3 == 0 and n:
                        pt_lo_copy(i, n // 3 - 1, 1)
                    if n % 3 == 1 and n > 3 and n < 24:
                        o_add(i, n // 3 - 1)
                    if n % 3 == 0 and n < 24:
                        st = n // 3
                        j, g = divmod(st, KV)
                        e = 6 * (STEPS * i + st)
                        heads = slice(GROUP * g, GROUP * (g + 1))
                        dve.wait_ge(scored, STEPS * i + st + 1)
                        dve.wait_ge(probs_turned, 2 * (STEPS * i + st))
                        table = 2 if j == 0 else j % 2
                        for h in range(GROUP):
                            last = dve.scalar_tensor_tensor(out=prob[:, h, :], in0=s.dist[:, table, :],
                                                            scalar=-SLOPE[GROUP * g + h], in1=score[:, h, :],
                                                            op0=ALU.mult, op1=ALU.add)
                        last.then_inc(soft_step, 1)
                        dve.wait_ge(soft_step, e + 1)
                        dve.tensor_reduce(neg_max[:], prob[:], AX.X, ALU.max, negate=True).then_inc(soft_step, 1)
                        dve.wait_ge(soft_step, e + 2)
                        dve.tensor_tensor(shift[:], neg_max[:], neg_sink[:, heads], ALU.min).then_inc(soft_step, 1)
                        dve.wait_ge(soft_step, e + 3)
                        dve.tensor_tensor(sink_in[:], shift[:], sink[:, heads], ALU.add).then_inc(shifted, 1)
                        if st == 1:
                            dve.tensor_copy(s.dist[:, 2, P:2 * P], s.dist[:, 0, P:2 * P]).then_inc(soft_step, 1)
                        else:
                            dve.sem_inc(soft_step, 1)
                    if n % 3 == 1 and n < 24:
                        st = n // 3
                        e = 6 * (STEPS * i + st)
                        dve.wait_ge(exped, 5 * (STEPS * i + st) + 5)
                        dve.wait_ge(normed, STEPS * i + st)
                        dve.tensor_tensor(denom[:], total[:], sink_e[:], ALU.add).then_inc(soft_step, 1)
                        dve.wait_ge(soft_step, e + 5)
                        dve.reciprocal(inv[:], denom[:]).then_inc(soft_step, 1)
                        dve.wait_ge(soft_step, e + 6)
                        dve.tensor_tensor(prob[:], prob[:], inv[:].unsqueeze(2).to_broadcast([P, GROUP, 2 * P]),
                                          ALU.mult).then_inc(normed, 1)
                        if st % 2 == 1 and st < STEPS - 1:
                            q_lo_block(QB * i + st // 2 + 1)
                    if n == SLOTS - 1:
                        o_add(i, STEPS - 1)

        @block.tensor
        def _(pe):
            def turn(i, x, xt):
                cols = GROUPS[xt][1]
                pe.wait_ge(group_out, NG * (5 * i + x) + xt + 1 + AHEAD)
                if x == K and xt == 0:
                    pe.wait_ge(v_rows, NG * i)
                elif x == K or xt == 0:
                    pe.wait_ge(k_rows, NG * i + (xt if x == K else NG))
                else:
                    pe.wait_ge(v_rows, NG * i + xt)
                    pe.wait_ge(v_hi, 4 * i + min(xt, NSB))
                if x == V and xt == 0 or x == K and xt == 0:
                    pe.wait_ge(v_hi, 4 * i)
                for j in range(max(1, cols // P)):
                    r = min(cols, P)
                    src = raw[:, xt % 2, j * P:j * P + r] if xt < NSB else raw_s[:]
                    last = pe.transpose(turned_ps[0:r, j * P:(j + 1) * P], src, s.ident[:])
                last.then_inc(turned, 1)

            def take_scores(i, st):
                j, g = divmod(st, KV)
                b = QB * i + j
                pe.wait_ge(q_ready, b + 1)
                pe.wait_ge(k_ready, b + 1)
                pe.wait_ge(shifted, STEPS * i + st)
                for h in range(GROUP):
                    qh = qpart[:, GROUP * g + h, :]
                    pe.matmul(score[:, h, :], qh, khi[:, g].rearrange("p b k -> p (b k)"), start=True, stop=False)
                    last = pe.matmul(score[:, h, :], qh, klo[:, g].rearrange("p b k -> p (b k)"),
                                     start=False, stop=True)
                last.then_inc(scored, 1)

            def turn_probs(i, st, slot):
                pe.wait_ge(normed, STEPS * i + st + 1)
                pe.wait_ge(pt_lo_ready, 2 * (STEPS * i + st) + slot)
                for h in range(GROUP):
                    last = pe.transpose(pt_ps[:, h * P:(h + 1) * P], prob[:, h, slot * P:(slot + 1) * P], s.ident[:])
                last.then_inc(probs_turned, 1)

            def mix(i, st, slot):
                j, g = divmod(st, KV)
                pe.wait_ge(v_block_in, 16 * (QB * i + j + 1))
                pe.wait_ge(pt_lo_ready, 2 * (STEPS * i + st) + slot + 1)
                pe.wait_ge(o_ready, STEPS * i + st)
                pe.matmul(o_ps[:], vwin[:, slot, g, :], pt_hi[slot][:], start=(slot == 0), stop=False)
                pe.matmul(o_ps[:], vwin[:, slot, g, :], pt_lo[slot][:], start=False, stop=(slot == 1))\
                  .then_inc(mixed, 1)

            pe.wait_ge(start_done, 1)
            with pe.Fori(0, PAIRS) as i:
                for n in range(SLOTS):
                    u, t = divmod(n, NG)
                    t0, cols = GROUPS[t]
                    c = 5 * i + u
                    if t == 0:
                        pe.wait_ge(w.lo_ready, c + 1)
                    wait_bank(pe, group_out, NG * c, t)
                    if (u == K and t in (2, 3)) or (u == V and t in (0, 1)):
                        pe.wait_ge(k_lo_done, 4 * i + {(K, 2): 1, (K, 3): 2, (V, 0): 3, (V, 1): 4}[u, t])
                    project(pe, s, w, SETS[u], bank[BANK[t]][:, 0:cols], t0, cols).then_inc(group_ready, 1)
                    if turned_slot(n):
                        turn(i, *turned_slot(n))
                    if n % 3 == 2:
                        turn_probs(i, n // 3, 0)
                    if n % 3 == 0 and n:
                        mix(i, n // 3 - 1, 0)
                        turn_probs(i, n // 3 - 1, 1)
                    if n % 3 == 1 and n > 3:
                        mix(i, n // 3 - 1, 1)
                    if n == SLOTS - 1:
                        mix(i, STEPS - 1, 1)
                    if n % 3 == 0 and n < 24:
                        take_scores(i, n // 3)


class OutProjection:

    def __init__(self, nc, s, ctx, tag="p", weights=None, other=None):
        sb = lambda name, shape, dt=F32: ctx.enter_context(nc.sbuf_tensor(f"{tag}_{name}", shape, dt))
        sem = lambda name: ctx.enter_context(nc.semaphore(f"{tag}_{name}"))
        self.s = s
        self.o, self.gate, self.x = sb("o", [P, DT, P]), sb("gate", [P, DT, P]), sb("x", [P, D])
        self.mixed, self.y = sb("mixed", [P, DT, P]), sb("y", [P, D])
        self.m_hi, self.m_lo = sb("m_hi", [P, DT, P], F32R), sb("m_lo", [P, DT, P], F32R)
        self.gate_loaded, self.o_loaded, self.x_loaded, self.y_stored = (
            sem(name) for name in ("gate_loaded", "o_loaded", "x_loaded", "y_stored"))
        steps = ("sig", "silu", "mix_ready", "hi_ready", "lo_ready", "summed", "y_ready")
        if other:
            self.counts = other.counts
        else:
            self.counts = [sem(name) for name in steps]
        self.sig, self.silu, self.mix_ready, self.hi_ready, self.lo_ready, self.summed, self.y_ready = self.counts
        self.sets = 2 if weights else 1
        bank = lambda n: ctx.enter_context(nc.psum_tensor(f"{tag}_ps{n}", [P, D // 2], F32))
        if weights:
            self.w_hi, self.w_lo = weights.w_hi, weights.w_lo
            self.ps = [bank(0), bank(1)]
        else:
            self.w_hi, self.w_lo = sb("w_hi", [P, DT, D], F32R), sb("w_lo", [P, DT, D], F32R)
            self.w_in = [sem("w_in0"), sem("w_in1")]
            self.w_hi_ready, self.w_lo_ready = sem("w_hi_ready"), sem("w_lo_ready")
            self.ps = [bank(0)] * 2

    def used(self, eng, signal, r, each=1):
        if self.sets == 1:
            eng.wait_ge(signal, each * r)
        elif r >= 2:
            eng.wait_ge(signal, each * (r - 1))

    def loads(self, r):
        return (r if self.sets == 1 else r // 2) + 1

    def raw_w(self, e):
        return self.gate[:].rearrange("p a c -> p (a c)") if e == 0 else self.x[:]

    def load_w(self, sp, n, e):
        if not (isinstance(n, int) and n == 0):
            sp.wait_ge(self.w_lo_ready, n - 1)
        sp.dma_start(self.raw_w(e), self.s.w_out[:, n, :]).then_inc(self.w_in[e], 16)

    def split_w_hi(self, act, n, e, half):
        act.wait_ge(self.w_in[e], 16 * half + 16)
        act.activation(self.w_hi[:, n, :], self.raw_w(e), ACT.Copy).then_inc(self.w_hi_ready, 1)

    def split_w_lo(self, pool, n, e):
        pool.wait_ge(self.w_hi_ready, n + 1)
        pool.tensor_tensor(self.w_lo[:, n, :], self.raw_w(e), f32(self.w_hi[:, n, :]),
                           ALU.subtract).then_inc(self.w_lo_ready, 1)

    def load_gate(self, sp, r):
        sp.wait_ge(self.mix_ready, r)
        sp.wait_ge(self.w_lo_ready, DT)
        sp.dma_start(self.gate[:], self.s.gateT_all[:, :, bass.ds(P * r, P)]).then_inc(self.gate_loaded, 16)

    def load_o(self, sp, r):
        sp.wait_ge(self.mix_ready, r)
        sp.dma_start(self.o[:], self.s.oT_all[:, :, bass.ds(P * r, P)]).then_inc(self.o_loaded, 16)

    def load_x(self, sp, r):
        sp.wait_ge(self.y_ready, 2 * r)
        sp.dma_start(self.x[:], self.s.x_prompt[bass.ds(P * r, P), :]).then_inc(self.x_loaded, 16)

    def store(self, sp, r):
        sp.wait_ge(self.y_ready, 2 * r + 2)
        sp.dma_start(self.s.y_prompt[bass.ds(P * r, P), :], self.y[:]).then_inc(self.y_stored, 16)

    def sigmoid(self, act, r, cols=P):
        act.wait_ge(self.gate_loaded, 16 * self.loads(r))
        self.used(act, self.lo_ready, r)
        act.activation(self.mixed[:, :, 0:cols], self.gate[:, :, 0:cols], ACT.Sigmoid).then_inc(self.sig, 1)

    def gate_o(self, pool, r, cols=P):
        pool.wait_ge(self.sig, r + 1)
        pool.tensor_tensor(self.mixed[:, :, 0:cols], self.mixed[:, :, 0:cols], self.gate[:, :, 0:cols],
                           ALU.mult).then_inc(self.silu, 1)
        pool.wait_ge(self.silu, r + 1)
        pool.wait_ge(self.o_loaded, 16 * self.loads(r))
        pool.tensor_tensor(self.mixed[:, :, 0:cols], self.mixed[:, :, 0:cols], self.o[:, :, 0:cols],
                           ALU.mult).then_inc(self.mix_ready, 1)

    def split_hi(self, act, r, cols=P):
        act.wait_ge(self.mix_ready, r + 1)
        self.used(act, self.summed, r, 2)
        act.activation(self.m_hi[:, :, 0:cols], self.mixed[:, :, 0:cols], ACT.Copy).then_inc(self.hi_ready, 1)

    def split_lo(self, dve, r, cols=P):
        dve.wait_ge(self.hi_ready, r + 1)
        dve.tensor_tensor(self.m_lo[:, :, 0:cols], self.mixed[:, :, 0:cols], f32(self.m_hi[:, :, 0:cols]),
                          ALU.subtract).then_inc(self.lo_ready, 1)

    def products(self, pe, r, half, tiles):
        cols = slice(half * D // 2, (half + 1) * D // 2)
        if tiles[0] == 0:
            pe.wait_ge(self.lo_ready, r + 1)
            if self.sets == 1:
                pe.wait_ge(self.y_ready, 2 * r + half)
            else:
                self.used(pe, self.y_ready, r, 2)
        for dt in tiles:
            pe.matmul(self.ps[half][:], self.m_hi[:, dt, :], self.w_hi[:, dt, cols], start=(dt == 0), stop=False)
            pe.matmul(self.ps[half][:], self.m_hi[:, dt, :], self.w_lo[:, dt, cols], start=False, stop=False)
            last = pe.matmul(self.ps[half][:], self.m_lo[:, dt, :], self.w_hi[:, dt, cols], start=False,
                             stop=(dt == DT - 1))
        if tiles[-1] == DT - 1:
            last.then_inc(self.summed, 1)

    def residual(self, dve, r, half, cols=P):
        c = slice(half * D // 2, (half + 1) * D // 2)
        dve.wait_ge(self.summed, 2 * r + half + 1)
        dve.wait_ge(self.x_loaded, 16 * self.loads(r))
        dve.wait_ge(self.y_stored, 16 * (self.loads(r) - 1))
        dve.tensor_tensor(self.y[0:cols, c], self.ps[half][0:cols, :], self.x[0:cols, c], ALU.add).then_inc(self.y_ready, 1)


def stick_breaking_stage(nc, s, proj):
    with ExitStack() as ctx:
        sb = lambda name, shape, dt=F32: ctx.enter_context(nc.sbuf_tensor(name, shape, dt))
        sem = lambda name: ctx.enter_context(nc.semaphore(name))
        qraw = [sb(f"c_qraw{e}", [P, SB]) for e in range(2)]
        q_hi = [sb(f"c_q_hi{e}", [P, SB], F32R) for e in range(2)]
        q_lo = [sb(f"c_q_lo{e}", [P, SB], F32R) for e in range(2)]
        k = [sb(f"c_k{e}", [P, NSB, SB], F32R) for e in range(2)]
        v = [sb(f"c_v{e}", [P, NSB, QB, P], F32R) for e in range(2)]
        keep = sb("c_keep", [P, 2, SB + 4])
        take = sb("c_take", [P, QB, SB])
        weight = sb("c_weight", [P, 2, QB, SB])
        kept = sb("c_kept", [P, QB, SB + 4])
        w_hi = [sb(f"c_w_hi{n}", [P, SB], F32R) for n in range(QB)]
        w_lo = [sb(f"c_w_lo{n}", [P, SB], F32R) for n in range(QB)]
        o_sum = [sb(f"c_o_sum{n}", [P, SB]) for n in range(2)]
        score = [ctx.enter_context(nc.psum_tensor(f"c_score{h}", [P, SB], F32)) for h in range(2)]
        turn_ps = [ctx.enter_context(nc.psum_tensor(f"c_turn{h}", [P, SB], F32)) for h in range(QB)]
        o_ps = ctx.enter_context(nc.psum_tensor("c_o", [P, SB], F32))
        q_in, k_in, v_in = ([sem(f"c_{n}{e}") for e in range(2)] for n in ("q_in", "k_in", "v_in"))
        new_slot_in = {q: sem(f"c_new_slot_in{q}") for q in range(1, NSB)}
        q_hi_ready, q_lo_ready, start_done = sem("c_q_hi_ready"), sem("c_q_lo_ready"), sem("c_start_done")
        scored, keep_ready, take_ready, scanned, weighted = (
            sem("c_" + n) for n in ("scored", "keep_ready", "take_ready", "scanned", "weighted"))
        turned, hi_ready, lo_ready, mixed = (sem("c_" + n) for n in ("turned", "hi_ready", "lo_ready", "mixed"))
        o_lo_out, o_ready, o_stored = sem("c_o_lo_out"), sem("c_o_ready"), [sem("c_o_stored0"), sem("c_o_stored1")]
        block = ctx.enter_context(nc.Block())

        units = lambda q, p: 4 * q * (q + 1) + 2 * (q + 1) * p
        heads = lambda q, p: HEADS * q + 2 * p
        loads = lambda q, p: 1 + 2 * q * (q + 1) + (q + 1) * p

        class Step:
            def __init__(self, q, p, u):
                self.q, self.p = q, p
                per = q + 1
                self.ahead = u // (2 * per)
                self.e = (u // per) % 2
                self.slot = u % per
                self.diagonal = self.slot == 0
                self.last = self.slot == q
                self.number = units(q, p) + u
                self.head = heads(q, p) + 2 * self.ahead + self.e
                self.head_e = 4 * q + p + self.ahead
                self.loads = loads(q, p) + (per if self.ahead else 0)
                self.par = u % 2

        def step_after(q, p, u, last):
            steps = 2 * (q + 1)
            if last and u >= steps:
                return Step(q + 1, 0, u - steps) if q < NSB - 1 else None
            return Step(q, p, u)

        def width(st, j):
            return P * (j + 1) if st.diagonal else SB

        def q_due(q, p, u, last):
            st = step_after(q, p, u + 3, last)
            return st if st and st.diagonal else None

        def projection_tiles(q, u, s):
            if q == 0:
                return []
            each, start = {1: (3, 10), 2: (2, 12), 3: (1, 12)}[q]
            first = (4 * u + s - start) * each
            return [divmod(n, DT) for n in range(first, first + each) if 0 <= n < 2 * DT]

        def iterations(eng, body):
            for q in range(NSB):
                with eng.Fori(0, PAIRS - 1) as p:
                    body(q, p, False)
                body(q, PAIRS - 1, True)

        @block.sync
        def _(sp):
            def load_q(q, p, e, nth):
                sp.wait_ge(q_lo_ready, nth)
                n = 4 * q + p
                for half in range(2):
                    sp.dma_start(qraw[e][half * HD:(half + 1) * HD, :],
                                 s.qT_all[bass.ds(n, 1), e * HD:(e + 1) * HD, :]
                                 .rearrange("o d t -> (o d) t")).then_inc(q_in[e], 16)

            def load_k(q, p, e, slots, signals):
                for slot in slots:
                    n = HEADS * (q - slot) + 2 * p + e
                    sp.dma_start(f32(k[e][:, slot, :]), s.k_parts_all[bass.ds(n, 1), :, :]
                                 .rearrange("o p c -> (o p) c")).then_inc(signals, 16)

            def load_v(q, p, e, slots, signals):
                for slot in slots:
                    n = HEADS * (q - slot) + 2 * p + e
                    sp.dma_start(f32(v[e][:, slot]).rearrange("p j c -> p (j c)"),
                                 s.v_parts_all[bass.ds(n, 1), :, :].rearrange("o p c -> (o p) c")).then_inc(signals, 16)

            def next_k(q, p, e):
                sp.wait_ge(scored, 4 * (units(q, p) + (e + 1) * (q + 1)))
                load_k(q, p + 1, e, range(q + 1), k_in[e])

            def body(q, p, last):
                end = last and q == NSB - 1
                if q == 0 and not last:
                    for e in range(2):
                        load_q(q, p + 2, e, heads(q, p + 1) + e + 1)
                elif q and not end:
                    for e in range(2):
                        load_q(q, p + 1, e, heads(q, p) + e + 1)
                if not q:
                    proj.load_w(sp, 2 * p + 1, 1)
                for e in range(2):
                    if q == 0 and not last:
                        next_k(q, p + 1, e)
                    elif q and not end:
                        next_k(q, p, e)
                    r = 4 * (q - 1) + p
                    if q and e == 0 and not end:
                        proj.load_gate(sp, r + 1)
                        if not last:
                            proj.load_o(sp, r + 1)
                    if q and e == 1:
                        proj.store(sp, r)
                        if not end:
                            proj.load_x(sp, r + 1)
                    if not q and not last and e == 1:
                        proj.load_w(sp, 2 * p + 2, 0)
                    sp.wait_ge(mixed, 4 * (units(q, p) + (e + 1) * (q + 1)))
                    if not end:
                        load_v(q, p + 1, e, range(q + 1), v_in[e])
                    sp.wait_ge(o_ready, heads(q, p) + e + 1)
                    sp.dma_start(s.oT_heads[bass.ds(2 * p + e, 1), :, SB * q:SB * (q + 1)]
                                 .rearrange("o d t -> (o d) t"), o_sum[e][0:HD, :]).then_inc(o_stored[e], 16)

            for e in range(2):
                load_q(0, 0, e, 0)
                load_k(0, 0, e, [0], k_in[e])
            proj.load_w(sp, 0, 0)
            for e in range(2):
                load_q(0, 1, e, e + 1)
                next_k(0, 0, e)
                load_v(0, 0, e, [0], v_in[e])
            for q in range(NSB):
                if q < NSB - 1:
                    for e in range(2):
                        load_k(q + 1, 0, e, [q + 1], new_slot_in[q + 1])
                        load_v(q + 1, 0, e, [q + 1], new_slot_in[q + 1])
                if q == 1:
                    proj.load_gate(sp, 0)
                    proj.load_x(sp, 0)
                if q:
                    for e in range(2):
                        sp.wait_ge(o_stored[e], 16 * PAIRS * q)
                    proj.load_o(sp, 4 * (q - 1))
                with sp.Fori(0, PAIRS - 1) as p:
                    body(q, p, False)
                body(q, PAIRS - 1, True)
            for e in range(2):
                sp.wait_ge(o_stored[e], 16 * NSB * PAIRS)
            sp.wait_ge(proj.y_stored, 16 * PAIRS * (NSB - 1))

        @block.gpsimd
        def _(pool):
            def q_lo_part(st):
                pool.wait_ge(q_hi_ready, st.head + 1)
                pool.tensor_tensor(q_lo[st.e][:], qraw[st.e][:], f32(q_hi[st.e][:]), ALU.subtract)\
                    .then_inc(q_lo_ready, 1)

            def weigh(st, j, initial=False):
                pool.wait_ge(scanned, 4 * st.number + j + 1)
                pool.wait_ge(take_ready, 4 * st.number + j + 1)
                if j == 0 and not initial:
                    pool.wait_ge(turned, 4 * (st.number - 1))
                n = width(st, j)
                pool.tensor_tensor(weight[:, st.par, j, 0:n], take[:, j, 0:n],
                                   kept[:, j, 1:n + 1], ALU.mult).then_inc(weighted, 1)

            def body(q, p, last):
                for u in range(2 * (q + 1)):
                    following, nxt = step_after(q, p, u + 1, last), step_after(q, p, u + 2, last)
                    due = q_due(q, p, u, last)
                    if following:
                        weigh(following, 1)
                        weigh(following, 2)
                    if q == 1 and u == 1:
                        proj.gate_o(pool, 4 * (q - 1) + p)
                    if following:
                        weigh(following, 3)
                    if due:
                        q_lo_part(due)
                    if nxt:
                        weigh(nxt, 0)
                    if q >= 2 and u == 1:
                        proj.gate_o(pool, 4 * (q - 1) + p)
                    if not q:
                        proj.split_w_lo(pool, 2 * p + u, u)

            pool.wait_ge(start_done, 1)
            for u in range(3):
                q_lo_part(Step(0, 0, u))
            for j in range(QB):
                weigh(Step(0, 0, 0), j, initial=True)
            weigh(Step(0, 0, 1), 0, initial=True)
            iterations(pool, body)

        @block.scalar
        def _(act):
            def q_hi_part(st, between, initial=False):
                act.wait_ge(q_in[st.e], 32 * (st.head_e + 1))
                if not initial:
                    act.wait_ge(scored, 4 * (st.number - between))
                act.activation(q_hi[st.e][:], qraw[st.e][:], ACT.Copy).then_inc(q_hi_ready, 1)

            def sigmoids(st, j, initial=False):
                n = width(st, j)
                act.wait_ge(scored, 4 * st.number + j + 1)
                if not initial or j > 1:
                    act.wait_ge(scanned, 4 * st.number + j - 1)
                act.activation(keep[:, j % 2, 0:n], score[j % 2][:, 0:n], ACT.Sigmoid, scale=-SCALE)\
                   .then_inc(keep_ready, 1)
                if not initial:
                    act.wait_ge(weighted, 4 * st.number + j - 3)
                act.activation(take[:, j, 0:n], score[j % 2][:, 0:n], ACT.Sigmoid, scale=SCALE)\
                   .then_inc(take_ready, 1)

            def back_hi(st, u, n):
                act.wait_ge(turned, 4 * st.number + n + 1)
                act.wait_ge(mixed, 4 * st.number + (n - 3 if u else 0))
                c = slice(P * n if st.diagonal else 0, SB)
                act.activation(w_hi[n][:, c], turn_ps[n][:, c], ACT.Copy).then_inc(hi_ready, 1)

            def finish(st):
                act.wait_ge(mixed, 4 * st.number + 4)
                act.wait_ge(o_stored[st.e], 16 * st.head_e)
                act.activation(o_sum[st.e][HD:P, :], o_ps[HD:P, :], ACT.Copy).then_inc(o_lo_out, 1)

            def body(q, p, last):
                for u in range(2 * (q + 1)):
                    st, nxt = Step(q, p, u), step_after(q, p, u + 2, last)
                    due = q_due(q, p, u, last)
                    back_hi(st, u, 0)
                    if nxt:
                        sigmoids(nxt, 0)
                    if q >= 2 and u == 1:
                        proj.sigmoid(act, 4 * (q - 1) + p)
                    if q == 1 and u == 2:
                        proj.split_hi(act, 4 * (q - 1) + p)
                    back_hi(st, u, 1)
                    if nxt:
                        sigmoids(nxt, 1)
                    if q >= 2 and u == 2:
                        proj.split_hi(act, 4 * (q - 1) + p)
                    if due:
                        q_hi_part(due, due.q + 1 if due.e else q + 1)
                    back_hi(st, u, 2)
                    if nxt:
                        sigmoids(nxt, 2)
                    if not q:
                        proj.split_w_hi(act, 2 * p + u, u, p)
                    if u and Step(q, p, u - 1).last:
                        finish(Step(q, p, u - 1))
                    back_hi(st, u, 3)
                    if nxt:
                        sigmoids(nxt, 3)
                    if q == 1 and u == 0:
                        proj.sigmoid(act, 4 * (q - 1) + p)
                finish(st)

            act.wait_ge(start_done, 1)
            for u in range(2):
                q_hi_part(Step(0, 0, u), 0, initial=True)
            for j in range(QB):
                sigmoids(Step(0, 0, 0), j, initial=True)
            q_hi_part(Step(0, 0, 2), 1)
            for j in range(QB):
                sigmoids(Step(0, 0, 1), j)
            iterations(act, body)

        @block.vector
        def _(dve):
            def scan(st, j, initial=False):
                dve.wait_ge(keep_ready, 4 * st.number + j + 1)
                if not initial:
                    dve.wait_ge(weighted, 4 * st.number + j - 3)
                    dve.wait_ge(scanned, 4 * st.number + j - 3)
                n = width(st, j) + (0 if st.diagonal else 1)
                down = slice(n - 1, None, -1)
                above = 1.0 if st.diagonal else kept[:, j, 0:1]
                dve.tensor_tensor_scan(kept[:, j, down], keep[:, j % 2, down], keep[:, j % 2, down], above,
                                       ALU.mult, ALU.bypass).then_inc(scanned, 1)

            def back_lo(st, n):
                dve.wait_ge(hi_ready, 4 * st.number + n + 1)
                c = slice(P * n if st.diagonal else 0, SB)
                dve.tensor_tensor(w_lo[n][:, c], turn_ps[n][:, c], f32(w_hi[n][:, c]),
                                  ALU.subtract).then_inc(lo_ready, 1)

            def finish(st):
                dve.wait_ge(o_lo_out, st.head + 1)
                dve.tensor_tensor(o_sum[st.e][0:HD, :], o_ps[0:HD, :], o_sum[st.e][HD:P, :],
                                  ALU.add).then_inc(o_ready, 1)

            def body(q, p, last):
                r = 4 * (q - 1) + p
                for u in range(2 * (q + 1)):
                    st, following, nxt = Step(q, p, u), step_after(q, p, u + 1, last), step_after(q, p, u + 2, last)
                    for n in range(QB):
                        if n == 0 and following:
                            scan(following, 3)
                        if n and nxt:
                            scan(nxt, n - 1)
                        if n == 3 and u and Step(q, p, u - 1).last:
                            finish(Step(q, p, u - 1))
                        back_lo(st, n)
                        if q and u == 2 and n == (0 if q == 1 else 1):
                            proj.split_lo(dve, r)
                        for half in range(2):
                            if (half, DT - 1) in projection_tiles(q, u, n):
                                proj.residual(dve, r, half)
                finish(st)

            dve.memset(keep[:], 1.0)
            dve.memset(kept[:], 1.0).then_inc(start_done, 1)
            dve.wait_ge(start_done, 1)
            for j in range(QB):
                scan(Step(0, 0, 0), j, initial=True)
            for j in range(QB - 1):
                scan(Step(0, 0, 1), j)
            iterations(dve, body)

        @block.tensor
        def _(pe):
            def front(st, j, first=False):
                if not first or j > 1:
                    pe.wait_ge(take_ready, 4 * st.number + j - 1)
                if j == 0:
                    if st.diagonal:
                        pe.wait_ge(q_lo_ready, st.head + 1)
                        pe.wait_ge(k_in[st.e], 16 * st.loads)
                    elif st.slot == st.q:
                        pe.wait_ge(new_slot_in[st.q], 64)
                n = width(st, j)
                out, keys = score[j % 2][:, 0:n], k[st.e][:, st.slot, 0:n]
                pe.matmul(out, q_hi[st.e][:, P * j:P * j + P], keys, start=True, stop=False)
                last = pe.matmul(out, q_lo[st.e][:, P * j:P * j + P], keys, start=False, stop=not st.diagonal)
                if st.diagonal:
                    last = pe.matmul(score[j % 2][:, n - P:n], s.ident_r[:], s.causal_r[:], start=False, stop=True)
                last.then_inc(scored, 1)

            def turn(st, u, n):
                if n == 0:
                    pe.wait_ge(weighted, 4 * st.number + 4)
                if u:
                    pe.wait_ge(lo_ready, 4 * st.number + n - 3)
                for j in range(n if st.diagonal else 0, QB):
                    last = pe.transpose(turn_ps[n][:, j * P:(j + 1) * P],
                                        weight[:, st.par, j, n * P:(n + 1) * P], s.ident[:])
                last.then_inc(turned, 1)

            def mix(st, n):
                pe.wait_ge(lo_ready, 4 * st.number + n + 1)
                if n == 0 and st.diagonal:
                    pe.wait_ge(o_ready, st.head)
                if n == 0 and st.diagonal:
                    pe.wait_ge(v_in[st.e], 16 * st.loads)
                c = slice(P * n if st.diagonal else 0, SB)
                end = st.last and n == QB - 1
                pe.matmul(o_ps[:, c], v[st.e][:, st.slot, n, :], w_hi[n][:, c],
                          start=(st.diagonal and n == 0), stop=False)
                pe.matmul(o_ps[:, c], v[st.e][:, st.slot, n, :], w_lo[n][:, c],
                          start=False, stop=end).then_inc(mixed, 1)

            def body(q, p, last):
                for u in range(2 * (q + 1)):
                    st, nxt = Step(q, p, u), step_after(q, p, u + 2, last)
                    for n in range(QB):
                        late = n == 3 and u and Step(q, p, u - 1).last
                        if n < 3 and u:
                            mix(Step(q, p, u - 1), n + 1)
                        if n == 3 and not late:
                            mix(st, 0)
                        turn(st, u, n)
                        if nxt:
                            front(nxt, n)
                        if late:
                            mix(st, 0)
                        for half, tile in projection_tiles(q, u, n):
                            proj.products(pe, 4 * (q - 1) + p, half, [tile])
                for n in range(1, QB):
                    mix(st, n)

            pe.wait_ge(start_done, 1)
            for u in range(2):
                for j in range(QB):
                    front(Step(0, 0, u), j, first=(u == 0))
            iterations(pe, body)


def sample_stage(nc, s):
    with ExitStack() as ctx:
        sb = lambda name, shape, dt=F32: ctx.enter_context(nc.sbuf_tensor(name, shape, dt))
        sem = lambda name: ctx.enter_context(nc.semaphore(name))
        PB = PAST // P
        NK = PAST + NS
        krows, vrows = sb("s_krows", [P, PB, HEADS * HD]), sb("s_vrows", [P, PB, HEADS * HD])
        vnew = sb("s_vnew", [NS, HEADS * HD])
        kT = sb("s_kT", [P, PAIRS, NK])
        qblk = sb("s_qblk", [P, PAIRS, P])
        mask = sb("s_mask", [P, NS])
        znew = sb("s_znew", [P, 2, NS])
        take, keep = sb("s_take", [P, 2, NK]), sb("s_keep", [P, 2, NK])
        kept = sb("s_kept", [P, 2, NK + 1])
        wT = sb("s_wT", [P, 2, PB + 1, P])
        oT = sb("s_oT", [P, PAIRS, NS])
        wk_rows, wv_rows, wv_new = sb("s_wk_rows", [P, P]), sb("s_wv_rows", [P, P]), sb("s_wv_new", [NS, P])
        wkT_last = sb("s_wkT_last", [P, P])
        wkT = sb("s_wkT", [P, WINDOW + NS])
        wq = sb("s_wq", [P, KV, P])
        out_rows, out_new = sb("s_out_rows", [P, P]), sb("s_out_new", [NS, P])
        dist = sb("s_dist", [NS, WINDOW + NS])
        prob = sb("s_prob", [P, KV, WINDOW + NS])
        probT, probT_new = sb("s_probT", [P, KV * P]), sb("s_probT_new", [NS, KV * P])
        sinks = sb("s_sinks", [P, HEADS])
        o_win = sb("s_o_win", [P, P])
        sink, neg_sink, neg_max, shift, sink_in, total, sink_e, denom, inv = (
            sb("s_" + n, [P, KV]) for n in ("sink", "neg_sink", "neg_max", "shift", "sink_in", "total",
                                            "sink_e", "denom", "inv"))
        turn = [ctx.enter_context(nc.psum_tensor(f"s_turn{c}", [P, SB], F32)) for c in range(PAIRS)]
        z = [ctx.enter_context(nc.psum_tensor(f"s_z{g}", [P, SB], F32)) for g in range(2)]
        z_new = ctx.enter_context(nc.psum_tensor("s_z_new", [P, SB], F32))
        win = ctx.enter_context(nc.psum_tensor("s_win", [P, SB], F32))
        cleared, k_in, v_in, q_in, w_in = (sem("s_" + n) for n in ("cleared", "k_in", "v_in", "q_in", "w_in"))
        k_turned, kT_ready, mask_ready, scored, znew_ready, take_ready = (
            sem("s_" + n) for n in ("k_turned", "kT_ready", "mask_ready", "scored", "znew_ready", "take_ready"))
        keep_ready, scanned, weighted, w_turned, wT_ready, o_done, oT_ready = (
            sem("s_" + n) for n in ("keep_ready", "scanned", "weighted", "w_turned", "wT_ready", "o_done", "oT_ready"))
        win_turned, win_ready, win_scored, dist_ready = (
            sem("s_" + n) for n in ("win_turned", "win_ready", "win_scored", "dist_ready"))
        step, exped, prob_ready, prob_turned, probT_ready, win_done, o_win_ready = (
            sem("s_" + n) for n in ("step", "exped", "prob_ready", "prob_turned", "probT_ready", "win_done",
                                    "o_win_ready"))
        stored = sem("s_stored")
        block = ctx.enter_context(nc.Block())

        @block.sync
        def _(sp):
            sp.dma_start(krows[:], s.cache_k).then_inc(k_in, 16)
            sp.dma_start(kT[:, :, PAST:NK], s.kT_sample.rearrange("c p t -> p c t")).then_inc(q_in, 16)
            sp.wait_ge(cleared, 1)
            for e in range(2):
                for c in range(2):
                    col = (2 * c + e) * NS
                    rows = slice(e * HD, (e + 1) * HD)
                    sp.dma_start(qblk[rows, c::2, col:col + NS],
                                 s.qT_sample[c::2, rows, :].rearrange("c p t -> p c t")).then_inc(q_in, 16)
            sp.dma_start(wk_rows[:], s.cache_win_k).then_inc(w_in, 16)
            sp.dma_start(wkT_last[:], s.normT[PAIRS, :, T - WINDOW:T]).then_inc(w_in, 16)
            sp.dma_start(wkT[:, WINDOW:], s.normT[PAIRS, :, T:TT]).then_inc(w_in, 16)
            for g in range(KV):
                rows = slice(g * HD, (g + 1) * HD)
                sp.dma_start(wq[rows, g, :].rearrange("p (h t) -> p h t", h=GROUP),
                             s.normT_q[:, GROUP * g:GROUP * (g + 1), T:TT]).then_inc(w_in, 16)
            sp.dma_start(sinks[:], s.attn_sink.to_broadcast([P, HEADS])).then_inc(w_in, 16)
            sp.dma_start(vrows[:], s.cache_v).then_inc(v_in, 16)
            sp.dma_start(vnew[:], s.sb_v_sample).then_inc(v_in, 16)
            sp.dma_start(wv_rows[:], s.cache_win_v).then_inc(v_in, 16)
            sp.dma_start(wv_new[:], s.win_v_rows[T:TT, :]).then_inc(v_in, 16)
            sp.dma_start(s.win_v_prompt, s.win_v_rows[T - WINDOW:T, :]).then_inc(stored, 16)
            sp.dma_start(s.win_k_sample[0:WINDOW - NS, :], s.cache_win_k[NS:WINDOW, :]).then_inc(stored, 16)
            sp.dma_start(s.win_v_sample[0:WINDOW - NS, :], s.cache_win_v[NS:WINDOW, :]).then_inc(stored, 16)
            sp.dma_start(s.win_v_sample[WINDOW - NS:WINDOW, :], s.win_v_rows[T:TT, :]).then_inc(stored, 16)
            sp.wait_ge(win_ready, 3)
            sp.dma_start(s.win_k_prompt, out_rows[:]).then_inc(stored, 16)
            sp.dma_start(s.win_k_sample[WINDOW - NS:WINDOW, :], out_new[:]).then_inc(stored, 16)
            sp.wait_ge(oT_ready, 4)
            sp.dma_start(s.oT[0:PAIRS, :, T:TT].rearrange("c p t -> p c t"), oT[:]).then_inc(stored, 16)
            sp.wait_ge(o_win_ready, 2)
            for g in range(KV):
                sp.dma_start(s.oT_win[g, :, :, T:TT], o_win[g * HD:(g + 1) * HD, :]
                             .rearrange("p (h t) -> p h t", h=GROUP)).then_inc(stored, 16)
            sp.wait_ge(stored, 9 * 16)

        @block.gpsimd
        def _(pool):
            for g in range(2):
                pool.wait_ge(scanned, g + 1)
                pool.tensor_tensor(take[:, g], take[:, g], kept[:, g, 1:], ALU.mult).then_inc(weighted, 1)

        @block.scalar
        def _(act):
            for c in range(0, PAIRS, 2):
                act.wait_ge(k_turned, c + 1)
                act.activation(kT[:, c, 0:PAST], turn[c][:], ACT.Copy).then_inc(kT_ready, 1)
            for g in range(2):
                act.wait_ge(scored, g + 1)
                act.activation(take[:, g, 0:PAST], z[g][:], ACT.Sigmoid, scale=SCALE).then_inc(take_ready, 1)
                act.wait_ge(znew_ready, g + 1)
                act.activation(take[:, g, PAST:], znew[:, g], ACT.Sigmoid, scale=SCALE).then_inc(take_ready, 1)
            for g in range(KV):
                act.wait_ge(step, 3 * g + 3)
                act.activation(prob[:, g], prob[:, g], ACT.Exp, bias=shift[:, g:g + 1],
                               accum_out=total[:, g:g + 1]).then_inc(exped, 1)
                act.activation(sink_e[:, g:g + 1], sink_in[:, g:g + 1], ACT.Exp).then_inc(exped, 1)
            for g in range(2):
                act.wait_ge(w_turned, g + 1)
                act.activation(wT[:, g, 0:PB, :].rearrange("p b k -> p (b k)"), turn[g][:], ACT.Copy)\
                   .then_inc(wT_ready, 1)
                act.activation(wT[0:NS, g, PB, :], turn[2 + g][0:NS, 0:P], ACT.Copy).then_inc(wT_ready, 1)

        @block.vector
        def _(dve):
            dve.memset(qblk[:], 0.0)
            dve.memset(wq[:], 0.0)
            dve.memset(kept[:], 1.0).then_inc(cleared, 1)
            for h in range(GROUP):
                last = dve.tensor_copy(mask[h * NS:(h + 1) * NS, :], s.causal[0:NS, 0:NS])
            last.then_inc(mask_ready, 1)
            dve.tensor_copy(dist[:, 0:WINDOW], s.dist[0:NS, 0, P:2 * P])
            dve.tensor_copy(dist[:, WINDOW:], s.dist[0:NS, 0, 0:NS]).then_inc(dist_ready, 1)
            for c in range(1, PAIRS, 2):
                dve.wait_ge(k_turned, c + 1)
                dve.tensor_copy(kT[:, c, 0:PAST], turn[c][:]).then_inc(kT_ready, 1)
            dve.wait_ge(win_turned, 1)
            dve.tensor_copy(wkT[:, 0:WINDOW], win[:, 0:P]).then_inc(win_ready, 1)
            dve.tensor_copy(out_rows[:], win[:, P:2 * P]).then_inc(win_ready, 1)
            dve.tensor_copy(out_new[:], win[0:NS, 2 * P:3 * P]).then_inc(win_ready, 1)
            dve.wait_ge(mask_ready, 1)
            dve.wait_ge(scored, 2)
            for g in range(2):
                dve.tensor_tensor(znew[:, g], z_new[:, g * NS:(g + 1) * NS], mask[:], ALU.add).then_inc(znew_ready, 1)
            dve.wait_ge(w_in, 6 * 16)
            for h in range(GROUP):
                rows = slice(h * NS, (h + 1) * NS)
                last = dve.tensor_copy(sink[rows, :], sinks[rows, h::GROUP])
            last.then_inc(dist_ready, 1)
            dve.wait_ge(dist_ready, 2)
            dve.tensor_scalar(neg_sink[:], sink[:], -1.0, None, ALU.mult).then_inc(dist_ready, 1)
            dve.wait_ge(dist_ready, 3)

            def scan(g):
                dve.wait_ge(take_ready, 2 * g + 2)
                dve.tensor_scalar(keep[:, g], take[:, g], -1.0, 1.0, ALU.mult, ALU.add).then_inc(keep_ready, 1)
                dve.wait_ge(keep_ready, g + 1)
                dve.tensor_tensor_scan(kept[:, g, NK - 1::-1], keep[:, g, ::-1], keep[:, g, ::-1], 1.0,
                                       ALU.mult, ALU.bypass).then_inc(scanned, 1)

            dve.wait_ge(cleared, 1)
            for g in range(KV):
                dve.wait_ge(win_scored, KV)
                for h in range(GROUP):
                    rows = slice(h * NS, (h + 1) * NS)
                    col = P + g * (WINDOW + NS)
                    last = dve.scalar_tensor_tensor(out=prob[rows, g], in0=dist[:], scalar=-SLOPE[GROUP * g + h],
                                                    in1=z_new[rows, col:col + WINDOW + NS],
                                                    op0=ALU.mult, op1=ALU.add)
                last.then_inc(prob_ready, 1)
                dve.wait_ge(prob_ready, g + 1)
                gc = slice(g, g + 1)
                dve.tensor_reduce(neg_max[:, gc], prob[:, g], AX.X, ALU.max, negate=True).then_inc(step, 1)
                dve.wait_ge(step, 3 * g + 1)
                dve.tensor_tensor(shift[:, gc], neg_max[:, gc], neg_sink[:, gc], ALU.min).then_inc(step, 1)
                dve.wait_ge(step, 3 * g + 2)
                dve.tensor_tensor(sink_in[:, gc], shift[:, gc], sink[:, gc], ALU.add).then_inc(step, 1)
                scan(g)
            dve.wait_ge(exped, 4)
            dve.tensor_tensor(denom[:], total[:], sink_e[:], ALU.add).then_inc(step, 1)
            dve.wait_ge(step, 7)
            dve.reciprocal(inv[:], denom[:]).then_inc(step, 1)
            dve.wait_ge(step, 8)
            dve.tensor_tensor(prob[:], prob[:], inv[:].unsqueeze(2).to_broadcast([P, KV, WINDOW + NS]),
                              ALU.mult).then_inc(prob_ready, 1)
            dve.wait_ge(prob_turned, 1)
            dve.tensor_copy(probT[:], win[:, 0:KV * P]).then_inc(probT_ready, 1)
            dve.tensor_copy(probT_new[:], win[0:NS, KV * P:2 * KV * P]).then_inc(probT_ready, 1)
            dve.wait_ge(o_done, PAIRS)
            for c in range(PAIRS):
                for e in range(2):
                    col = P * c + (2 * (c % 2) + e) * NS
                    last = dve.tensor_copy(oT[e * HD:(e + 1) * HD, c, :], z[0][e * HD:(e + 1) * HD, col:col + NS])
                last.then_inc(oT_ready, 1)
            dve.wait_ge(win_done, KV)
            for g in range(KV):
                rows = slice(g * HD, (g + 1) * HD)
                dve.tensor_copy(o_win[rows, :], z[1][rows, g * P:(g + 1) * P]).then_inc(o_win_ready, 1)

        @block.tensor
        def _(pe):
            pe.wait_ge(k_in, 16)
            for c in range(PAIRS):
                for b in range(PB):
                    last = pe.transpose(turn[c][:, b * P:(b + 1) * P], krows[:, b, c * P:(c + 1) * P], s.ident[:])
                last.then_inc(k_turned, 1)
            pe.wait_ge(w_in, 6 * 16)
            pe.transpose(win[:, 0:P], wk_rows[:], s.ident[:])
            pe.transpose(win[:, P:2 * P], wkT_last[:], s.ident[:])
            pe.transpose(win[0:NS, 2 * P:3 * P], wkT[:, WINDOW:], s.ident[:]).then_inc(win_turned, 1)
            pe.wait_ge(kT_ready, 4)
            pe.wait_ge(q_in, 5 * 16)
            for g in range(2):
                for c in range(2):
                    pe.matmul(z[g][:], qblk[:, 2 * g + c], kT[:, 2 * g + c, 0:PAST], start=(c == 0), stop=(c == 1))
                for c in range(2):
                    last = pe.matmul(z_new[:, g * NS:(g + 1) * NS], qblk[:, 2 * g + c], kT[:, 2 * g + c, PAST:],
                                     start=(c == 0), stop=(c == 1))
                last.then_inc(scored, 1)
            pe.wait_ge(win_ready, 3)
            pe.wait_ge(znew_ready, 2)
            for g in range(KV):
                col = P + g * (WINDOW + NS)
                pe.matmul(z_new[:, col:col + WINDOW + NS], wq[:, g], wkT[:], start=True, stop=True).then_inc(win_scored, 1)
            for g in range(2):
                pe.wait_ge(weighted, g + 1)
                for b in range(PB):
                    pe.transpose(turn[g][:, b * P:(b + 1) * P], take[:, g, b * P:(b + 1) * P], s.ident[:])
                pe.transpose(turn[2 + g][0:NS, 0:P], take[:, g, PAST:], s.ident[:]).then_inc(w_turned, 1)
            pe.wait_ge(prob_ready, 3)
            for g in range(KV):
                pe.transpose(win[:, g * P:(g + 1) * P], prob[:, g, 0:WINDOW], s.ident[:])
                last = pe.transpose(win[0:NS, (KV + g) * P:(KV + g + 1) * P], prob[:, g, WINDOW:], s.ident[:])
            last.then_inc(prob_turned, 1)
            pe.wait_ge(v_in, 4 * 16)
            pe.wait_ge(take_ready, 4)
            for c in range(PAIRS):
                g = c // 2
                pe.wait_ge(wT_ready, 2 * g + 2)
                out = z[0][:, P * c:P * (c + 1)]
                for b in range(PB):
                    pe.matmul(out, vrows[:, b, c * P:(c + 1) * P], wT[:, g, b, :], start=(b == 0), stop=False)
                pe.matmul(out, vnew[:, c * P:(c + 1) * P], wT[0:NS, g, PB, :], start=False, stop=True).then_inc(o_done, 1)
            pe.wait_ge(probT_ready, 2)
            for g in range(KV):
                cols = slice(g * P, (g + 1) * P)
                pe.matmul(z[1][:, cols], wv_rows[:], probT[:, cols], start=True, stop=False)
                pe.matmul(z[1][:, cols], wv_new[:], probT_new[:, cols], start=False, stop=True).then_inc(win_done, 1)


def tail_stage(nc, s, weights):
    with ExitStack() as ctx:
        sets = [OutProjection(nc, s, ctx, "t0", weights)]
        sets.append(OutProjection(nc, s, ctx, "t1", weights, other=sets[0]))
        first = PAIRS * (NSB - 1)
        turns = [(sets[n % 2], n, first + n, P if first + n < T // P else NS) for n in range(QB + 1)]
        block = ctx.enter_context(nc.Block())

        @block.sync
        def _(sp):
            def load(proj, n, row, cols):
                t0 = P * row
                proj.used(sp, proj.mix_ready, n)
                sp.dma_start(proj.gate[:, :, 0:cols], s.gateT_all[:, :, t0:t0 + cols])\
                  .then_inc(proj.gate_loaded, 16)
                sp.dma_start(proj.o[:, :, 0:cols], s.oT_all[:, :, t0:t0 + cols]).then_inc(proj.o_loaded, 16)

            def load_x(proj, n, row, cols):
                proj.used(sp, proj.y_ready, n, 2)
                src = s.x_prompt[P * row:P * row + cols, :] if cols == P else s.x_sample
                sp.dma_start(proj.x[0:cols, :], src).then_inc(proj.x_loaded, 16)

            load(*turns[0])
            load(*turns[1])
            load_x(*turns[0])
            load_x(*turns[1])
            for i, (proj, n, row, cols) in enumerate(turns):
                if i + 2 < len(turns):
                    load(*turns[i + 2])
                sp.wait_ge(proj.y_ready, 2 * n + 2)
                dst = s.y_prompt[P * row:P * row + cols, :] if cols == P else s.y_sample
                sp.dma_start(dst, proj.y[0:cols, :]).then_inc(proj.y_stored, 16)
                if i + 2 < len(turns):
                    load_x(*turns[i + 2])
            sp.wait_ge(sets[0].y_stored, 16 * 3)
            sp.wait_ge(sets[1].y_stored, 16 * 2)

        @block.gpsimd
        def _(pool):
            for proj, n, row, cols in turns:
                proj.gate_o(pool, n, cols)

        @block.scalar
        def _(act):
            for i, (proj, n, row, cols) in enumerate(turns):
                if i == 0:
                    proj.sigmoid(act, n, cols)
                if i + 1 < len(turns):
                    turns[i + 1][0].sigmoid(act, turns[i + 1][1], turns[i + 1][3])
                proj.split_hi(act, n, cols)

        @block.vector
        def _(dve):
            for i, (proj, n, row, cols) in enumerate(turns):
                if i == 0:
                    proj.split_lo(dve, n, cols)
                if i + 1 < len(turns):
                    turns[i + 1][0].split_lo(dve, turns[i + 1][1], turns[i + 1][3])
                proj.residual(dve, n, 0, cols)
                proj.residual(dve, n, 1, cols)

        @block.tensor
        def _(pe):
            for proj, n, row, cols in turns:
                proj.products(pe, n, 0, range(DT))
                proj.products(pe, n, 1, range(DT))


INPUTS = ["x_prompt", "x_sample", "cache_sb_k", "cache_sb_v", "cache_win_k", "cache_win_v",
          "norm_g", "w_in", "q_norm_g", "k_norm_g", "attn_sink", "w_out"]
OUTPUTS = [("y_prompt", (1, T, D)), ("y_sample", (1, NS, D)),
           ("sb_k_prompt", (1, 1, T, HEADS, HD)), ("sb_v_prompt", (1, 1, T, HEADS, HD)),
           ("win_k_prompt", (1, 1, WINDOW, KV, HD)), ("win_v_prompt", (1, 1, WINDOW, KV, HD)),
           ("sb_k_sample", (1, 1, NS, HEADS, HD)), ("sb_v_sample", (1, 1, NS, HEADS, HD)),
           ("win_k_sample", (1, 1, WINDOW, KV, HD)), ("win_v_sample", (1, 1, WINDOW, KV, HD))]


def build(nc, args, stages=99):
    s = Shared()
    s.x_prompt = args["x_prompt"].rearrange("b t d -> (b t) d")
    s.x_sample = args["x_sample"].rearrange("b t d -> (b t) d")
    s.norm_g, s.q_norm_g, s.k_norm_g, s.attn_sink = (args[n] for n in ("norm_g", "q_norm_g", "k_norm_g", "attn_sink"))
    s.w_in = args["w_in"].rearrange("o (a p) n -> (o p) a n", p=P)
    dram = lambda name, shape, dt=F32: nc.dram_tensor(name, shape, dt, kind="Internal").ap()
    s.normT = dram("normT", [5, P, TT])
    s.win_v_rows = dram("win_v_rows", [TT, P])
    s.win_v_parts = dram("win_v_parts", [NSB, P, QB * KV * P])
    s.normT_q = s.normT[0:PAIRS].rearrange("c (e d) t -> d (c e) t", d=HD)
    s.normT_k = s.normT[PAIRS].rearrange("(g d) t -> d g t", d=HD)
    s.qT = dram("qT", [NSB, PAIRS, P, SB])
    s.qT_sample = dram("qT_sample", [PAIRS, P, NS])
    s.kT_sample = dram("kT_sample", [PAIRS, P, NS])
    s.gateT = dram("gateT", [DT, P, TT])
    s.oT = dram("oT", [DT, P, TT])
    s.oT_win = s.oT[PAIRS:DT].rearrange("(g c) (e d) t -> g d (c e) t", g=KV, d=HD)
    s.k_parts = dram("k_parts", [NSB, HEADS, P, SB])
    s.v_parts = dram("v_parts", [NSB, HEADS, P, SB])
    s.sb_k_rows, s.sb_v_rows = (args[n].rearrange("o b (s j p) h d -> s p (o b j) (h d)", p=P, j=QB)
                                for n in ("sb_k_prompt", "sb_v_prompt"))
    s.sb_k_sample, s.sb_v_sample = (args[n].rearrange("o b t h d -> (o b t) (h d)") for n in ("sb_k_sample", "sb_v_sample"))
    s.w_out = args["w_out"].rearrange("o (a p) n -> (o p) a n", p=P)
    s.oT_all, s.gateT_all = s.oT.rearrange("a p t -> p a t"), s.gateT.rearrange("a p t -> p a t")
    s.y_prompt, s.y_sample = (args[n].rearrange("b t d -> (b t) d") for n in ("y_prompt", "y_sample"))
    s.qT_all = s.qT.rearrange("s c p t -> (s c) p t")
    s.k_parts_all, s.v_parts_all = (a.rearrange("s h p c -> (s h) p c") for a in (s.k_parts, s.v_parts))
    s.oT_heads = s.oT[0:PAIRS].rearrange("c (e d) t -> (c e) d t", d=HD)
    s.cache_k, s.cache_v = (args[n].rearrange("o b (j p) h d -> p (o b j) (h d)", p=P)
                            for n in ("cache_sb_k", "cache_sb_v"))
    s.cache_win_k, s.cache_win_v, s.win_k_prompt, s.win_v_prompt, s.win_k_sample, s.win_v_sample = (
        args[n].rearrange("o b t h d -> (o b t) (h d)") for n in (
            "cache_win_k", "cache_win_v", "win_k_prompt", "win_v_prompt", "win_k_sample", "win_v_sample"))
    with ExitStack() as ctx:
        keep = lambda name, shape, dt=F32: ctx.enter_context(nc.sbuf_tensor(name, shape, dt))
        s.ident = keep("ident", [P, P])
        s.ident_r = keep("ident_r", [P, P], F32R)
        s.causal = keep("causal", [P, P])
        s.causal_r = keep("causal_r", [P, P], F32R)
        s.ones_head = keep("ones_head", [P, P])
        s.eps = keep("eps", [P, 1])
        s.qk_gain = keep("qk_gain", [P, 2])
        s.dist = keep("dist", [P, 3, 2 * P])
        s.dist_ready = ctx.enter_context(nc.semaphore("dist_ready"))
        with ExitStack() as ctx_x:
            s.XH = ctx_x.enter_context(nc.sbuf_tensor("XH", [P, DT, TT], F32R))
            s.XL = ctx_x.enter_context(nc.sbuf_tensor("XL", [P, DT, TT], F32R))
            norm_stage(nc, s, ctx_x)
            if stages > 1:
                window_project_stage(nc, s)
            if stages > 2:
                pair_project_stage(nc, s)
        if stages > 4:
            sample_stage(nc, s)
        with ExitStack() as ctx_c:
            proj = OutProjection(nc, s, ctx_c)
            if stages > 3:
                stick_breaking_stage(nc, s, proj)
            if stages > 4:
                tail_stage(nc, s, proj)


def kernel(x_prompt, x_sample, cache_sb_k, cache_sb_v, cache_win_k, cache_win_v, norm_g, w_in,
           q_norm_g, k_norm_g, attn_sink, w_out):
    import numpy as np
    from concourse import bacc
    from concourse.bass_utils import run_bass_kernel_spmd

    arrays = dict(zip(INPUTS, map(np.asarray, (x_prompt, x_sample, cache_sb_k, cache_sb_v, cache_win_k, cache_win_v,
                                               norm_g, w_in, q_norm_g, k_norm_g, attn_sink, w_out))))
    nc = bacc.Bacc("TRN2", target_bir_lowering=False, num_devices=1)
    args = {n: nc.dram_tensor(f"in_{n}", a.shape, F32, kind="ExternalInput").ap() for n, a in arrays.items()}
    args.update({n: nc.dram_tensor(f"out_{n}", shape, F32, kind="ExternalOutput").ap() for n, shape in OUTPUTS})
    build(nc, args)
    result = run_bass_kernel_spmd(nc, [{f"in_{n}": a for n, a in arrays.items()}], core_ids=[0])
    return tuple(np.asarray(result.results[0][f"out_{n}"]) for n, _ in OUTPUTS)
```
